# Optimizing a Trainium2 kernel written in Bass

```python
import math
import jax, jax.numpy as jnp
from jax import lax
import numpy as np

D_MODEL = 2048
BATCH = 1
SEQ = 256
DEPTH = 1
DEC_BATCH = 8
DEC_SEQ = 4
PAST_LEN = 2048
PAGE_SIZE = 128

N_META = 16
D_ATTN = D_MODEL // 2
N_HEADS = 8
HEAD_DIM = D_ATTN // (2 * N_HEADS)
D_CONV = D_MODEL - D_ATTN
CONV_W = 31
D_FF = 4 * D_MODEL
D_IN = 3 * D_ATTN + 2 * D_CONV
Q_BLOCK = 128
EPS = 1e-6
NEG_INF = -1e30

kernel_name = "hymba_diffattn_conformer_step"

def lambda_init(l):
    return 0.8 - 0.6 * math.exp(-0.3 * l)

def rms_norm(x, g):
    xf = x.astype(jnp.float32)
    y = xf * lax.rsqrt(jnp.mean(xf * xf, axis=-1, keepdims=True) + EPS) * g.astype(jnp.float32)
    return y.astype(x.dtype)

def diff_lambda(l, lambda_q1, lambda_k1, lambda_q2, lambda_k2):
    f32 = jnp.float32
    return (jnp.exp(jnp.sum(lambda_q1[l].astype(f32) * lambda_k1[l].astype(f32)))
            - jnp.exp(jnp.sum(lambda_q2[l].astype(f32) * lambda_k2[l].astype(f32)))
            + lambda_init(l))

def diff_attn_core(q, k, v, q_pos, k_pos, lam):
    s = jnp.einsum('bqhd,bkhd->bhqk', q.astype(jnp.float32), k.astype(jnp.float32)) * (HEAD_DIM ** -0.5)
    s = jnp.where(k_pos[None, :] <= q_pos[:, None], s, NEG_INF)
    p = jax.nn.softmax(s, axis=-1)
    b, _, lq, lk = p.shape
    p = p.reshape(b, N_HEADS, 2, lq, lk)
    a = p[:, :, 0] - lam * p[:, :, 1]
    return jnp.einsum('bhqk,bkhe->bqhe', a, v.astype(jnp.float32))

def attend_prompt(q, k, v, lam):
    b, L = q.shape[:2]
    pos = jnp.arange(L)
    o_meta = diff_attn_core(q[:, :N_META], k[:, :N_META], v[:, :N_META], pos[:N_META], pos[:N_META], lam)
    nb = (L - N_META) // Q_BLOCK
    qb = q[:, N_META:].reshape(b, nb, Q_BLOCK, 2 * N_HEADS, HEAD_DIM).transpose(1, 0, 2, 3, 4)
    pb = pos[N_META:].reshape(nb, Q_BLOCK)
    ob = lax.map(lambda a: diff_attn_core(a[0], k, v, a[1], pos, lam), (qb, pb))
    o_real = ob.transpose(1, 0, 2, 3, 4).reshape(b, L - N_META, N_HEADS, 2 * HEAD_DIM)
    return jnp.concatenate([o_meta, o_real], axis=1)

def conformer_conv(u, prev, dw_w, dw_b, ln_g, ln_b):
    a, g = jnp.split(u, 2, axis=-1)
    h = a * jax.nn.sigmoid(g)
    ext = jnp.concatenate([prev.astype(h.dtype), h], axis=1)
    c = lax.conv_general_dilated(ext, dw_w[:, None, :].astype(ext.dtype), (1,), 'VALID',
                                 dimension_numbers=('NWC', 'WIO', 'NWC'),
                                 feature_group_count=D_CONV)
    cf = c.astype(jnp.float32) + dw_b.astype(jnp.float32)
    mu = jnp.mean(cf, axis=-1, keepdims=True)
    var = jnp.mean(jnp.square(cf - mu), axis=-1, keepdims=True)
    cn = (cf - mu) * lax.rsqrt(var + EPS) * ln_g.astype(jnp.float32) + ln_b.astype(jnp.float32)
    return jax.nn.silu(cn).astype(u.dtype), ext[:, -(CONV_W - 1):]

def project_in(x, l, attn_norm, w_in, q_norm, k_norm):
    b, L = x.shape[:2]
    z = rms_norm(x, attn_norm[l]) @ w_in[l]
    q = z[..., :D_ATTN].reshape(b, L, 2 * N_HEADS, HEAD_DIM)
    k = z[..., D_ATTN:2 * D_ATTN].reshape(b, L, 2 * N_HEADS, HEAD_DIM)
    v = z[..., 2 * D_ATTN:3 * D_ATTN].reshape(b, L, N_HEADS, 2 * HEAD_DIM)
    u = z[..., 3 * D_ATTN:]
    return rms_norm(q, q_norm[l]), rms_norm(k, k_norm[l]), v, u

def finish_layer(x, o_attn, c_out, l, attn_subln, w_out, mlp_norm, w_up, w_down):
    b, L = x.shape[:2]
    oa = (rms_norm(o_attn, attn_subln[l]) * (1.0 - lambda_init(l))).astype(x.dtype).reshape(b, L, D_ATTN)
    x = x + jnp.concatenate([oa, c_out], axis=-1) @ w_out[l]
    h = rms_norm(x, mlp_norm[l]) @ w_up[l]
    return x + jnp.square(jax.nn.relu(h)) @ w_down[l]

def setup_inputs(seed: int = 0) -> dict:
    key = jax.random.key(seed)
    ks = jax.random.split(key, 24)
    f32 = jnp.float32
    n_pages = PAST_LEN // PAGE_SIZE
    n_used = DEC_BATCH * n_pages
    n_phys = n_used + max(1, n_used // 4)
    nrm = lambda k, s, sc: jax.random.normal(k, s, f32) * sc
    page_table = jax.random.permutation(ks[5], n_phys)[:n_used].reshape(DEC_BATCH, n_pages).astype(jnp.int32)
    return {
        "x_prompt": nrm(ks[0], (BATCH, SEQ, D_MODEL), 1.0),
        "x_sample": nrm(ks[1], (DEC_BATCH, DEC_SEQ, D_MODEL), 1.0),
        "cache_k": nrm(ks[2], (DEPTH, n_phys, PAGE_SIZE, 2 * N_HEADS, HEAD_DIM), 1.0),
        "cache_v": nrm(ks[3], (DEPTH, n_phys, PAGE_SIZE, N_HEADS, 2 * HEAD_DIM), 1.0),
        "state_conv": nrm(ks[4], (DEPTH, DEC_BATCH, CONV_W - 1, D_CONV), 0.5),
        "page_table": page_table,
        "meta_tokens": nrm(ks[6], (N_META, D_MODEL), 1.0),
        "attn_norm": 1.0 + nrm(ks[7], (DEPTH, D_MODEL), 0.02),
        "w_in": nrm(ks[8], (DEPTH, D_MODEL, D_IN), D_MODEL ** -0.5),
        "q_norm": 1.0 + nrm(ks[9], (DEPTH, HEAD_DIM), 0.02),
        "k_norm": 1.0 + nrm(ks[10], (DEPTH, HEAD_DIM), 0.02),
        "lambda_q1": nrm(ks[11], (DEPTH, HEAD_DIM), 0.1),
        "lambda_k1": nrm(ks[12], (DEPTH, HEAD_DIM), 0.1),
        "lambda_q2": nrm(ks[13], (DEPTH, HEAD_DIM), 0.1),
        "lambda_k2": nrm(ks[14], (DEPTH, HEAD_DIM), 0.1),
        "attn_subln": 1.0 + nrm(ks[15], (DEPTH, 2 * HEAD_DIM), 0.02),
        "dw_w": nrm(ks[16], (DEPTH, CONV_W, D_CONV), CONV_W ** -0.5),
        "dw_b": nrm(ks[17], (DEPTH, D_CONV), 0.02),
        "conv_ln_g": 1.0 + nrm(ks[18], (DEPTH, D_CONV), 0.02),
        "conv_ln_b": nrm(ks[19], (DEPTH, D_CONV), 0.02),
        "w_out": nrm(ks[20], (DEPTH, D_ATTN + D_CONV, D_MODEL), (D_ATTN + D_CONV) ** -0.5),
        "mlp_norm": 1.0 + nrm(ks[21], (DEPTH, D_MODEL), 0.02),
        "w_up": nrm(ks[22], (DEPTH, D_MODEL, D_FF), D_MODEL ** -0.5),
        "w_down": nrm(ks[23], (DEPTH, D_FF, D_MODEL), D_FF ** -0.5),
    }

def reference(x_prompt, x_sample, cache_k, cache_v, state_conv, page_table, meta_tokens,
              attn_norm, w_in, q_norm, k_norm, lambda_q1, lambda_k1, lambda_q2, lambda_k2,
              attn_subln, dw_w, dw_b, conv_ln_g, conv_ln_b, w_out, mlp_norm, w_up, w_down):
    b = x_prompt.shape[0]
    meta = jnp.broadcast_to(meta_tokens.astype(x_prompt.dtype)[None], (b, N_META, D_MODEL))
    x = jnp.concatenate([meta, x_prompt], axis=1)
    kp, vp, cp = [], [], []
    for l in range(DEPTH):
        lam = diff_lambda(l, lambda_q1, lambda_k1, lambda_q2, lambda_k2)
        q, k, v, u = project_in(x, l, attn_norm, w_in, q_norm, k_norm)
        o = attend_prompt(q, k, v, lam)
        c, cs = conformer_conv(u, jnp.zeros((b, CONV_W - 1, D_CONV), u.dtype),
                               dw_w[l], dw_b[l], conv_ln_g[l], conv_ln_b[l])
        kp.append(k); vp.append(v); cp.append(cs)
        x = finish_layer(x, o, c, l, attn_subln, w_out, mlp_norm, w_up, w_down)
    y_prompt = x[:, N_META:]

    db, ds = x_sample.shape[:2]
    past_len = page_table.shape[1] * cache_k.shape[2]
    q_pos = past_len + jnp.arange(ds)
    k_pos = jnp.arange(past_len + ds)
    xs = x_sample
    ks_, vs_, cs_ = [], [], []
    for l in range(DEPTH):
        lam = diff_lambda(l, lambda_q1, lambda_k1, lambda_q2, lambda_k2)
        q, k, v, u = project_in(xs, l, attn_norm, w_in, q_norm, k_norm)
        k_past = cache_k[l][page_table].reshape(db, past_len, 2 * N_HEADS, HEAD_DIM)
        v_past = cache_v[l][page_table].reshape(db, past_len, N_HEADS, 2 * HEAD_DIM)
        k_all = jnp.concatenate([k_past.astype(k.dtype), k], axis=1)
        v_all = jnp.concatenate([v_past.astype(v.dtype), v], axis=1)
        o = diff_attn_core(q, k_all, v_all, q_pos, k_pos, lam)
        c, cs = conformer_conv(u, state_conv[l], dw_w[l], dw_b[l], conv_ln_g[l], conv_ln_b[l])
        ks_.append(k); vs_.append(v); cs_.append(cs)
        xs = finish_layer(xs, o, c, l, attn_subln, w_out, mlp_norm, w_up, w_down)
    y_sample = xs

    return (y_prompt, y_sample, jnp.stack(kp), jnp.stack(vp), jnp.stack(cp),
            jnp.stack(ks_), jnp.stack(vs_), jnp.stack(cs_))


_drawn_inputs = setup_inputs


def setup_inputs(seed=0):
    import zlib

    import numpy as np

    out = dict(_drawn_inputs(seed))
    spreads = {}
    factors = {'q_norm': 4.788,
     'lambda_k2': 3.01,
     'attn_subln': 5.583,
     'dw_b': 3.783,
     'conv_ln_g': 6.409,
     'conv_ln_b': 7.408,
     'mlp_norm': 3.364}
    for name, (base, spread) in spreads.items():
        noise = np.random.default_rng([zlib.crc32(name.encode()), seed]).standard_normal(out[name].shape)
        drawn = base * np.exp(spread * noise) if base else spread * noise
        out[name] = __import__('jax').numpy.asarray(drawn.astype(out[name].dtype))
    for name, factor in factors.items():
        out[name] = (out[name] * factor).astype(out[name].dtype)
    return out
```

```python
from contextlib import ExitStack

import concourse.bass as bass
import concourse.mybir as mybir

F32 = mybir.dt.float32
F32R = mybir.dt.float32r
I32 = mybir.dt.int32
ALU = mybir.AluOpType
ACT = mybir.ActivationFunctionType
AX = mybir.AxisListType.X
ds = bass.ds

P = 128
EPS = 1e-6
NEG_INF = -1e30
LAMBDA_INIT = 0.2
N_META = 16
SEQ = 256
N_SEQ = 8
DEC = 4
N_SMP = N_SEQ * DEC
T_P = N_META + SEQ
T = T_P + N_SMP
T_OUT = T - N_META
D = 2048
KT = D // P
N_H = 8
HD = 64
D_ATTN = 1024
D_CONV = 1024
TAPS = 31
D_FF = 8192
D_IN = 3 * D_ATTN + 2 * D_CONV
N_PAGES = 16
VC = 512
MT = VC // P
CK = 2
NC = KT // CK
RAW = 4
SPL = 2
PG = 8
PAD = 16
ZW = PAD + T
QC = 2 * DEC
SC = N_H * QC
Q_V = D_IN // VC
Z_VISITS = 8
NORM_VISITS = 4
ATT_FIRST = 5
N_ATT_V = Q_V - ATT_FIRST
OUT_V0 = Q_V
OUT_N = D // VC
MLP_V0 = OUT_V0 + OUT_N
N_QTR = 4
FQ = D_FF // N_QTR
UP_N = FQ // VC
DOWN_N = D // VC
QTR_N = UP_N + DOWN_N
V_ATTN, V_MLP, V_DWB, V_LNG, V_LNB, V_SUB, V_Q, V_K = 0, 16, 32, 40, 48, 56, 57, 58
N_VEC = 59
KC_STORES = 4 + 1 + 2 * N_SEQ
CONSTS = 14
STATE = 16 * (N_SEQ + 1 + 4)
CV_S = 2 + 2 * TAPS + 1
TOK = [(0, 128), (128, 128), (256, 48)]
NAT = [(0, 128), (128, 128), (256, 16), (T_P, N_SMP)]


def build_step(nc, x_prompt, x_sample, cache_k, cache_v, state_conv, page_table, meta_tokens,
               attn_norm, w_in, q_norm, k_norm, lambda_q1, lambda_k1, lambda_q2, lambda_k2,
               attn_subln, dw_w, dw_b, conv_ln_g, conv_ln_b, w_out, mlp_norm, w_up, w_down,
               y_prompt, y_sample, k_prompt, v_prompt, conv_prompt, k_sample, v_sample, conv_sample):
    ctx = ExitStack()
    with ctx:
        def sb(name, shape, dt=F32):
            return ctx.enter_context(nc.sbuf_tensor(name, shape, dt))

        def aliased(*layouts):
            made = []
            for group in layouts[:-1]:
                with ExitStack() as part:
                    made.append([part.enter_context(nc.sbuf_tensor(*g)) for g in group])
            made.append([sb(*g) for g in layouts[-1]])
            return made

        def sem(name):
            return ctx.enter_context(nc.semaphore(name))

        ident = sb("ident", [P, P])
        ones = sb("ones", [P, P])
        head_ones = sb("head_ones", [P, P])
        causal = sb("causal", [P, P])
        new_mask = sb("new_mask", [N_SMP, N_SEQ, DEC])
        eps = sb("eps", [P, 1])
        vec = sb("vec", [P, N_VEC])
        qk_gain = sb("qk_gain", [P, 16])
        taps = sb("taps", [P, 8, TAPS])
        neg_lam = sb("neg_lam", [P, 1])
        lam_in = sb("lam_in", [1, 4, HD])
        lam_prod = sb("lam_prod", [1, 2, HD])
        lam_sum = sb("lam_sum", [1, 2])
        lam_exp = sb("lam_exp", [1, 2])
        lam_one = sb("lam_one", [1, 1])
        pages_sb = sb("pages_sb", [1, N_SEQ * N_PAGES], I32)
        xT = sb("xT", [P, KT, T])
        rstd = sb("rstd", [P, T])
        sums = sb("sums", [P, 3])
        root = sb("root", [P, 3])
        inv = sb("inv", [P, 3])
        tmp = sb("tmp", [P, MT, T])
        raw = sb("raw", [P, RAW, CK, VC])
        w_hi = sb("w_hi", [P, SPL, CK, VC], F32R)
        w_lo = sb("w_lo", [P, SPL, CK, VC], F32R)
        (v_nat, prob, probT), (a_hi, a_lo) = aliased(
            [("v_nat", [P, 4, D_ATTN], F32), ("prob", [P, 4, T_P], F32), ("probT", [P, 2, 3, P], F32)],
            [("a_hi", [P, KT, T], F32R), ("a_lo", [P, KT, T], F32R)])
        (h_hi, h_lo), (z,) = aliased(
            [("h_hi", [P, KT, T_OUT], F32R), ("h_lo", [P, KT, T_OUT], F32R)],
            [("z", [P, 32, ZW], F32)])
        (x_nat, st_nat), (k_nat, g_nat), (y_nat, y_smp), (page,) = aliased(
            [("x_nat", [P, 3, D], F32), ("st_nat", [120, 2, D_CONV], F32)],
            [("k_nat", [P, 4, D_ATTN], F32), ("g_nat", [P, 2, D_CONV], F32)],
            [("y_nat", [P, 2, D], F32), ("y_smp", [N_SMP, D], F32)],
            [("page", [P, PG, D_ATTN], F32)])
        (cw_nat, vec_nat), (kT,) = aliased(
            [("cw_nat", [TAPS, D_CONV], F32), ("vec_nat", [N_VEC, P], F32)],
            [("kT", [P, 2, N_H, P], F32)])
        (rb,), (S,) = aliased([("rb", [P, 3, P], F32)], [("S", [P, N_PAGES, SC], F32)])
        q_new = sb("q_new", [P, N_SEQ, N_H, QC])
        s_new = sb("s_new", [N_SMP, N_SEQ, N_H, QC])
        o_cache = sb("o_cache", [P, N_SEQ, SC])
        l_cache = sb("l_cache", [P, N_SEQ, SC])
        neg_max = sb("neg_max", [P, N_SEQ, SC])
        o_smp = sb("o_smp", [P, N_SEQ * N_H, DEC])
        pmax = sb("pmax", [P, P])
        lpart = sb("lpart", [P, SC])
        nm = sb("nm", [SC, 1])
        nm_diag = sb("nm_diag", [SC, SC])
        ext = sb("ext", [P, 8, N_SEQ, TAPS - 1 + DEC])
        c_smp = sb("c_smp", [P, 8, N_SEQ, DEC])
        c_prod = sb("c_prod", [P, 8, N_SEQ, DEC])
        pstat = sb("pstat", [P, 2, 4])

        acc = ctx.enter_context(nc.psum_tensor("acc", [P, MT, 512], F32))
        aux = ctx.enter_context(nc.psum_tensor("aux", [P, 4, 512], F32))

        x_in = [sem(f"x_in{t}") for t in range(3)]
        small_in = sem("small_in")
        state_in = sem("state_in")
        pages_in = sem("pages_in")
        raw_in = [sem(f"raw_in{r}") for r in range(RAW)]
        page_in = [sem(f"page_in{r}") for r in range(PG)]
        consts = sem("consts")
        x_turned = sem("x_turned")
        x_kept = sem("x_kept")
        a_hi_ok = sem("a_hi_ok")
        a_lo_ok = sem("a_lo_ok")
        set_t = sem("set_t")
        set_v = sem("set_v")
        sq_x = sem("sq_x")
        hi_ok = sem("hi_ok")
        lo_ok = sem("lo_ok")
        w_used = sem("w_used")
        acc_ok = sem("acc_ok")
        acc_free = sem("acc_free")
        nrm_sq = sem("nrm_sq")
        nrm_sum = sem("nrm_sum")
        nrm_root = sem("nrm_root")
        nrm_v = sem("nrm_v")
        q_ok = sem("q_ok")
        sn_mm = sem("sn_mm")
        sn_ok = sem("sn_ok")
        kT_mm = [sem("kT_mm0"), sem("kT_mm1")]
        kT_ok = [sem("kT_ok0"), sem("kT_ok1")]
        sc_mm = sem("sc_mm")
        sc_ok = sem("sc_ok")
        mx_v = sem("mx_v")
        mx_mm = sem("mx_mm")
        nm_ok = sem("nm_ok")
        sub_ok = sem("sub_ok")
        exp_ok = sem("exp_ok")
        lp_ok = sem("lp_ok")
        pv_mm = sem("pv_mm")
        l_mm = sem("l_mm")
        o_ok = sem("o_ok")
        l_ok = sem("l_ok")
        gate_e = sem("gate_e")
        gate_v = sem("gate_v")
        nat_mm = sem("nat_mm")
        nat_a = sem("nat_a")
        nat_d = sem("nat_d")
        lam_v = sem("lam_v")
        lam_a = sem("lam_a")
        lam_m = sem("lam_m")
        pa_s = sem("pa_s")
        pa_max = sem("pa_max")
        pa_exp = sem("pa_exp")
        pa_v = sem("pa_v")
        pa_t = sem("pa_t")
        pa_tc = sem("pa_tc")
        pa_o = sem("pa_o")
        pa_oc = sem("pa_oc")
        nw_v = sem("nw_v")
        nw_e = sem("nw_e")
        nw_m = sem("nw_m")
        sub_sq = sem("sub_sq")
        sub_mm = sem("sub_mm")
        sub_rt = sem("sub_rt")
        sub_v = sem("sub_v")
        cv_p = sem("cv_p")
        cv_s = sem("cv_s")
        ln_mm = sem("ln_mm")
        ln_v = sem("ln_v")
        ln_sq = sem("ln_sq")
        ln_rt = sem("ln_rt")
        ln_n = sem("ln_n")
        ln_s = sem("ln_s")
        ln_e = sem("ln_e")
        x2_sq = sem("x2_sq")
        x2_mm = sem("x2_mm")
        x2_rt = sem("x2_rt")
        x2_v = sem("x2_v")
        up_h = sem("up_h")
        h_hi_ok = sem("h_hi_ok")
        h_lo_ok = sem("h_lo_ok")
        y_mm = sem("y_mm")
        y_a = sem("y_a")
        y_d = sem("y_d")
        v_out = sem("v_out")
        kc_out = sem("kc_out")
        y_out = sem("y_out")

        kin, kout = cache_k[0], cache_v[0]
        k_pages = kin.rearrange("n p h d -> n p (h d)")
        v_pages = kout.rearrange("n p h d -> n p (h d)")
        st = state_conv[0]
        n_phys = k_pages.shape[0]
        xs_rows = x_sample.rearrange("b t d -> (b t) d")
        w_in2, w_out2, w_up2, w_down2 = w_in[0], w_out[0], w_up[0], w_down[0]

        def w_chunk(w, row, col):
            return w[ds(row, CK * P), ds(col, VC)].rearrange("(k p) n -> p k n", p=P)

        block = ctx.enter_context(nc.Block())

        @block.sync
        def _(sp):
            def load_w(n, j, src):
                sp.wait_ge(lo_ok, NC * n + j + 1)
                sp.dma_start(raw[:, j % RAW], src).then_inc(raw_in[j % RAW], 16)

            def w_src(n, j):
                return w_chunk(w_in2, CK * P * j, VC * n)

            def load_page(s, j, keys, wait=None):
                r = sp.value_load(pages_sb[0:1, ds(N_PAGES * s + j, 1)], min_val=0, max_val=n_phys - 1)
                src = k_pages if keys else v_pages
                if wait:
                    sp.wait_ge(*wait)
                sp.dma_start(page[:, j % PG], src[ds(r, 1)].rearrange("a p n -> p (a n)"))\
                  .then_inc(page_in[j % PG], 16)

            xp = x_prompt[0]
            sp.dma_start(x_nat[0:N_META, 0, :], meta_tokens).then_inc(x_in[0], 16)
            sp.dma_start(x_nat[N_META:P, 0, :], xp[0:P - N_META, :]).then_inc(x_in[0], 16)
            sp.dma_start(x_nat[:, 1, :], xp[P - N_META:2 * P - N_META, :]).then_inc(x_in[1], 16)
            sp.dma_start(x_nat[0:16, 2, :], xp[2 * P - N_META:SEQ, :]).then_inc(x_in[2], 16)
            sp.dma_start(x_nat[16:48, 2, :], xs_rows).then_inc(x_in[2], 16)
            for j in range(RAW):
                load_w(0, j, w_src(0, j))
            for j in range(RAW, NC):
                load_w(0, j, w_src(0, j))
            with sp.Fori(1, ATT_FIRST) as n:
                for j in range(NC):
                    load_w(n, j, w_src(n, j))
            sp.wait_ge(x_turned, KT)
            sp.wait_ge(set_t, 6)
            sp.wait_ge(sq_x, 3)
            sp.wait_ge(pages_in, 16)
            for j in range(PG):
                load_page(0, j, True)
            for j in range(RAW):
                load_w(ATT_FIRST, j, w_src(ATT_FIRST, j))

            def sequence(s, n, nxt, more):
                w_at = {0: 4, 4: 5, 8: 6, 12: 7, 16: 8, 18: 9, 20: 10, 24: 11}
                for i in range(2 * N_PAGES if more else 2 * N_PAGES - PG):
                    if n is not None and i in w_at:
                        j = w_at[i]
                        if j < NC:
                            load_w(n, j, w_src(n, j))
                        else:
                            load_w(n + 1, j - NC, nxt(n + 1, j - NC))
                    if i < PG:
                        load_page(s, i + PG, True, (kT_mm[1], N_PAGES * s + i + 1))
                    elif i < 2 * PG:
                        load_page(s, i - PG, False, (kT_mm[1], N_PAGES * s + i + 1))
                    elif i < 3 * PG:
                        load_page(s, i - PG, False, (pv_mm, N_PAGES * s + i - 2 * PG + 1))
                    else:
                        load_page(s + 1, i - 3 * PG, True, (pv_mm, N_PAGES * s + i - 2 * PG + 1))

            def w_out_src(n, j):
                return w_chunk(w_out2, CK * P * j, VC * (n - OUT_V0))

            with sp.Fori(0, N_ATT_V - 1) as s:
                sequence(s, s + ATT_FIRST, w_src, True)
            sequence(N_ATT_V - 1, Q_V - 1, w_out_src, True)
            with sp.Fori(N_ATT_V, N_SEQ - 1) as s:
                sequence(s, None, None, True)
            sequence(N_SEQ - 1, None, None, False)

            for j in range(RAW, NC):
                load_w(OUT_V0, j, w_out_src(OUT_V0, j))
            with sp.Fori(OUT_V0 + 1, MLP_V0) as n:
                for j in range(NC):
                    load_w(n, j, w_out_src(n, j))
            with sp.Fori(0, N_QTR) as q:
                with sp.Fori(0, UP_N) as u:
                    for j in range(NC):
                        load_w(MLP_V0 + q * QTR_N + u, j, w_chunk(w_up2, CK * P * j, q * FQ + u * VC))
                with sp.Fori(0, DOWN_N) as d:
                    for j in range(NC):
                        load_w(MLP_V0 + UP_N + q * QTR_N + d, j,
                               w_chunk(w_down2, q * FQ + CK * P * j, d * VC))
            for g in range(4):
                cols = slice(VC * g, VC * (g + 1))
                for i in range(3):
                    b = 3 * g + i
                    sp.wait_ge(y_a if b % 2 == 0 else y_d, b // 2 + 1)
                    if i < 2:
                        sp.dma_start(y_prompt[0, P * i:P * (i + 1), cols], y_nat[:, i, cols]).then_inc(y_out, 16)
                    else:
                        sp.dma_start(y_sample.rearrange("b t d -> (b t) d")[:, cols], y_smp[:, cols])\
                          .then_inc(y_out, 16)
            sp.wait_ge(y_out, 16 * 12)
            sp.wait_ge(v_out, 16 * 4)
            sp.wait_ge(kc_out, 16 * KC_STORES)

        @block.gpsimd
        def _(pool):
            def row(v):
                return v.rearrange("(a n) -> a n", n=P)
            pool.dma_start(vec_nat[V_ATTN:V_ATTN + 16, :], row(attn_norm[0])).then_inc(small_in, 16)
            pool.dma_start(vec_nat[V_MLP:V_MLP + 16, :], row(mlp_norm[0])).then_inc(small_in, 16)
            pool.dma_start(vec_nat[V_DWB:V_DWB + 8, :], row(dw_b[0])).then_inc(small_in, 16)
            pool.dma_start(vec_nat[V_LNG:V_LNG + 8, :], row(conv_ln_g[0])).then_inc(small_in, 16)
            pool.dma_start(vec_nat[V_LNB:V_LNB + 8, :], row(conv_ln_b[0])).then_inc(small_in, 16)
            pool.dma_start(vec_nat[V_SUB:V_SUB + 1, :], attn_subln).then_inc(small_in, 16)
            for half in range(2):
                pool.dma_start(vec_nat[V_Q:V_Q + 1, HD * half:HD * (half + 1)], q_norm).then_inc(small_in, 16)
                pool.dma_start(vec_nat[V_K:V_K + 1, HD * half:HD * (half + 1)], k_norm).then_inc(small_in, 16)
            pool.memset(ident[:], 0.0).then_inc(consts, 1)
            pool.memset(causal[:], 0.0).then_inc(consts, 1)
            pool.memset(new_mask[:], 0.0).then_inc(consts, 1)
            pool.memset(head_ones[:], 0.0).then_inc(consts, 1)
            pool.memset(ones[:], 1.0).then_inc(consts, 1)
            pool.memset(eps[:], EPS).then_inc(consts, 1)
            pool.wait_ge(consts, 6)
            pool.affine_select(out=ident[:], in_=ident[:], compare_op=ALU.not_equal, fill=1.0, base=0,
                               pattern=[[-1, P]], channel_multiplier=1).then_inc(consts, 1)
            pool.affine_select(out=causal[:], in_=causal[:], compare_op=ALU.is_ge, fill=NEG_INF, base=0,
                               pattern=[[-1, P]], channel_multiplier=1).then_inc(consts, 1)
            pool.affine_select(out=new_mask[:], in_=new_mask[:], compare_op=ALU.is_ge, fill=NEG_INF, base=0,
                               pattern=[[-DEC, N_SEQ], [0, DEC]], channel_multiplier=1).then_inc(consts, 1)
            pool.wait_ge(consts, 9)
            pool.memset(head_ones[0:HD, 0:HD], 1.0).then_inc(consts, 1)
            pool.wait_ge(consts, 10)
            pool.memset(head_ones[HD:P, HD:P], 1.0).then_inc(consts, 1)
            pool.wait_ge(consts, 11)
            pool.affine_select(out=new_mask[:], in_=new_mask[:], compare_op=ALU.is_ge, fill=NEG_INF, base=0,
                               pattern=[[DEC, N_SEQ], [1, DEC]], channel_multiplier=-1).then_inc(consts, 1)
            pool.memset(q_new[:], 0.0).then_inc(consts, 1)
            pool.memset(pmax[:], 0.0).then_inc(consts, 1)
            for b in range(2):
                for s in range(4):
                    pool.dma_start(st_nat[30 * s:30 * (s + 1), b, :], st[4 * b + s]).then_inc(state_in, 16)
            pool.dma_start(cw_nat[:, :], dw_w[0]).then_inc(state_in, 16)
            pool.dma_start(pages_sb[0:1, :], page_table.rearrange("s (a n) -> a (s n)", a=1)).then_inc(pages_in, 16)
            for i, v in enumerate((lambda_q1, lambda_q2, lambda_k1, lambda_k2)):
                pool.dma_start(lam_in[0:1, i, :], v).then_inc(state_in, 16)

            kp = k_prompt[0, 0].rearrange("t h d -> t (h d)")
            vp = v_prompt[0, 0].rearrange("t h d -> t (h d)")
            ks = k_sample[0].rearrange("b t h d -> (b t) (h d)")
            vs = v_sample[0].rearrange("b t h d -> (b t) (h d)")
            for s in range(N_SEQ):
                pool.dma_start(conv_sample[0, s, 0:TAPS - 1 - DEC, :], st[s, DEC:TAPS - 1, :]).then_inc(kc_out, 16)

            def store(which, buf, prompt, smp, signal):
                for i, (t0, n) in enumerate(NAT):
                    pool.wait_ge(nat_a, 4 * which + i + 1)
                    pool.wait_ge(nat_d, 4 * which + i + 1)
                    dst = prompt[t0:t0 + n, :] if i < 3 else smp
                    pool.dma_start(dst, buf[0:n, i, :]).then_inc(signal, 16)

            store(0, v_nat, vp, vs, v_out)
            pool.wait_ge(gate_v, 24)
            pool.wait_ge(set_v, 9)
            pool.tensor_copy(ext[:, :, :, TAPS - 1:], z[:, 24:32, PAD + T_P:ZW].rearrange("p c (s t) -> p c s t", t=DEC))\
                .then_inc(cv_s, 1)
            full = [P, 8, N_SEQ, DEC]
            bias = vec[:, V_DWB:V_DWB + 8].unsqueeze(2).unsqueeze(3).to_broadcast(full)
            pool.tensor_copy(c_smp[:], bias).then_inc(cv_s, 1)
            for j in range(TAPS):
                tap = taps[:, :, j:j + 1].unsqueeze(3).to_broadcast(full)
                pool.wait_ge(cv_s, 2 + 2 * j)
                pool.tensor_tensor(c_prod[:], ext[:, :, :, j:j + DEC], tap, ALU.mult).then_inc(cv_s, 1)
                pool.wait_ge(cv_s, 3 + 2 * j)
                pool.tensor_tensor(c_smp[:], c_smp[:], c_prod[:], ALU.add).then_inc(cv_s, 1)
            pool.wait_ge(cv_s, 2 + 2 * TAPS)
            pool.wait_ge(nat_mm, 8)
            pool.tensor_copy(z[:, 16:24, SEQ:T_OUT].rearrange("p c (s t) -> p c s t", t=DEC), c_smp[:])\
                .then_inc(cv_s, 1)

            store(1, k_nat, kp, ks, kc_out)
            pool.wait_ge(nat_a, 10)
            pool.wait_ge(nat_d, 10)
            pool.dma_start(conv_prompt[0, 0], g_nat[0:TAPS - 1, 0, :]).then_inc(kc_out, 16)
            for s in range(N_SEQ):
                pool.dma_start(conv_sample[0, s, TAPS - 1 - DEC:TAPS - 1, :], g_nat[DEC * s:DEC * s + DEC, 1, :])\
                    .then_inc(kc_out, 16)


        @block.tensor
        def _(pe):
            mm, transpose = nc.tensor.matmul, nc.tensor.transpose
            pe.sem_inc(sc_mm, 2)

            def products(n, kt, hi, lo, c0, width):
                slot = kt // CK % SPL
                if kt % CK == 0:
                    pe.wait_ge(lo_ok, RAW + NC * n + kt // CK + 1)
                for m in range(MT):
                    if kt == 0:
                        pe.wait_ge(acc_free, MT * n + m + 1)
                    wh = w_hi[:, slot, kt % CK, P * m:P * (m + 1)]
                    wl = w_lo[:, slot, kt % CK, P * m:P * (m + 1)]
                    ah, al = hi[:, kt, c0:c0 + width], lo[:, kt, c0:c0 + width]
                    out = acc[:, m, 0:width]
                    mm(out, wh, ah, start=(kt == 0), stop=False)
                    mm(out, wh, al, start=False, stop=False)
                    last = mm(out, wl, ah, start=False, stop=(kt == KT - 1))
                    if kt == KT - 1:
                        last.then_inc(acc_ok, 1)
                    elif kt % CK == CK - 1 and m == MT - 1:
                        last.then_inc(w_used, 1)

            pe.wait_ge(consts, CONSTS)
            pe.wait_ge(small_in, 160)
            transpose(aux[:, 0, 0:N_VEC], vec_nat[:, :], ident[0:N_VEC, 0:N_VEC]).then_inc(set_t, 1)
            for t in range(3):
                pe.wait_ge(x_in[t], 16 if t == 1 else 32)
            for kt in range(KT):
                if kt >= 4:
                    pe.wait_ge(x_kept, kt - 3)
                for t, (t0, n) in enumerate(TOK):
                    last = transpose(acc[:, kt % 4, t0:t0 + n], x_nat[0:n, t, P * kt:P * (kt + 1)],
                                     ident[0:n, 0:n])
                last.then_inc(x_turned, 1)
            pe.wait_ge(x_kept, KT)
            for kt in range(KT):
                pe.wait_ge(a_lo_ok, kt + 1)
                products(0, kt, a_hi, a_lo, 0, T)
                if kt == 3:
                    pe.wait_ge(state_in, STATE)
                    for c in range(8):
                        last = transpose(aux[:, 1, TAPS * c:TAPS * (c + 1)], cw_nat[:, P * c:P * (c + 1)],
                                         ident[0:TAPS, 0:TAPS])
                    last.then_inc(set_t, 1)
                    for g in range(4):
                        if g >= 2:
                            pe.wait_ge(set_v, 3 + g)
                        for c in range(4):
                            ch = 4 * (g % 2) + c
                            last = transpose(aux[:, (2, 3, 1, 2)[g], 120 * c:120 * (c + 1)],
                                             st_nat[:, g // 2, P * ch:P * (ch + 1)], ident[0:120, 0:120])
                        last.then_inc(set_t, 1)
                if kt == 8:
                    pe.wait_ge(set_v, 14)
                    for t, (t0, n) in enumerate(TOK):
                        last = mm(aux[:, 0, t0:t0 + n], rb[0:n, t, :], ident[0:n, 0:n], start=True, stop=True)
                    last.then_inc(set_t, 1)
            with pe.Fori(1, ATT_FIRST) as n:
                for kt in range(KT):
                    products(n, kt, a_hi, a_lo, 0, T)
                    if kt == 7:
                        for m in range(MT):
                            pe.wait_ge(nrm_sq, MT * (n - 1) + m + 1)
                            mm(aux[:, m, 0:T], head_ones[:], tmp[:, m, :], start=True, stop=True)\
                              .then_inc(nrm_sum, 1)
            pe.wait_ge(q_ok, 2)
            for h in range(N_H):
                last = mm(aux[0:N_SMP, 0, :].rearrange("p (s h c) -> p s h c", h=N_H, c=QC)[:, :, h, :],
                          z[:, 8 + h, PAD + T_P:PAD + T], q_new[:, :, h, :], start=True, stop=True)
            last.then_inc(sn_mm, 1)
            pe.wait_ge(sn_ok, 1)

            def turn_keys(s, j):
                pe.wait_ge(page_in[j % PG], 16 * (4 * s + j // PG + 1))
                for half in range(2):
                    pe.wait_ge(kT_ok[half], N_PAGES * s + j + 1)
                    for h in range(4):
                        last = transpose(aux[:, half, P * h:P * (h + 1)],
                                         page[:, j % PG, P * (4 * half + h):P * (4 * half + h + 1)], ident[:])
                    last.then_inc(kT_mm[half], 1)

            def score(s, j):
                pe.wait_ge(kT_ok[0], 1 + N_PAGES * s + j + 1)
                pe.wait_ge(kT_ok[1], 1 + N_PAGES * s + j + 1)
                if j == 0:
                    pe.wait_ge(l_ok, s + 1)
                else:
                    pe.wait_ge(sc_ok, N_PAGES * s + j)
                for h in range(N_H):
                    last = mm(aux[:, 2, QC * h:QC * (h + 1)], kT[:, j % 2, h, :],
                              q_new[:, ds(s, 1), h, :].rearrange("p a c -> p (a c)"), start=True, stop=True)
                last.then_inc(sc_mm, 1)

            def values(s, j):
                pe.wait_ge(page_in[j % PG], 16 * (4 * s + 2 + j // PG + 1))
                if j % 8 == 0:
                    pe.wait_ge(exp_ok, 2 * s + j // 8 + 1)
                if j == 0:
                    pe.wait_ge(o_ok, s + 1)
                for h in range(N_H):
                    last = mm(aux[:, 3, QC * h:QC * (h + 1)], page[:, j % PG, P * h:P * (h + 1)],
                              S[:, j, QC * h:QC * (h + 1)], start=(j == 0 and h == 0),
                              stop=(j == N_PAGES - 1), skip_group_check=True)
                last.then_inc(pv_mm, 1)

            def sequence(s, n):
                kt = iter(range(KT))

                def visit(count=1):
                    if n is not None:
                        for _ in range(count):
                            products(n, next(kt), a_hi, a_lo, 0, T)
                for j in range(N_PAGES):
                    turn_keys(s, j)
                    if j in (1, 4, 6, 9, 11, 14):
                        visit()
                    if j >= 1:
                        score(s, j - 1)
                score(s, N_PAGES - 1)
                visit()
                pe.wait_ge(mx_v, 4 * s + 2)
                transpose(aux[:, 2, P:2 * P], pmax[:], ident[:]).then_inc(mx_mm, 1)
                visit()
                pe.wait_ge(mx_v, 4 * s + 4)
                mm(aux[:, 2, 2 * P:2 * P + SC], ones[0:SC, :], nm_diag[:], start=True, stop=True).then_inc(mx_mm, 1)
                visit(2)
                for j in range(N_PAGES):
                    values(s, j)
                    if j in (1, 4, 6, 9, 11, 14):
                        visit()
                pe.wait_ge(lp_ok, s + 1)
                mm(aux[:, 2, 3 * P:3 * P + SC], ones[:], lpart[:], start=True, stop=True).then_inc(l_mm, 1)

            with pe.Fori(0, N_ATT_V) as s:
                sequence(s, s + ATT_FIRST)
            pe.wait_ge(acc_free, MT * (Q_V + 1))
            pe.wait_ge(gate_v, 24)
            b = 0
            for base, parts in ((16, NAT), (8, NAT), (24, ((T_P - 30, 30), (T_P, N_SMP)))):
                if base == 8:
                    with pe.Fori(N_ATT_V, N_SEQ) as s:
                        sequence(s, None)
                for t0, n in parts:
                    for half in range(2):
                        if b >= 4:
                            pe.wait_ge(nat_a if b % 2 == 0 else nat_d, (b - 4) // 2 + 1)
                        for h in range(4):
                            last = transpose(acc[0:n, b % 4, P * h:P * (h + 1)],
                                             z[:, base + 4 * half + h, PAD + t0:PAD + t0 + n], ident[:])
                        last.then_inc(nat_mm, 1)
                        b += 1
            pe.wait_ge(nat_a, 10)
            pe.wait_ge(nat_d, 10)
            pe.wait_ge(lam_v, 4)
            pe.wait_ge(l_ok, 1 + N_SEQ)
            mm(aux[:, 2, 0:1], ones[0:1, :], lam_one[0:1, :], start=True, stop=True).then_inc(lam_m, 1)
            pe.wait_ge(lam_v, 5)

            def p_score(u):
                h, blk = u // 2, u % 2
                nk = N_META + P * (blk + 1)
                if u >= 2:
                    pe.wait_ge(pa_exp, 2 * (u - 1))
                for i in range(2):
                    rows = slice(HD * i, HD * (i + 1))
                    q0 = PAD + N_META + P * blk
                    for k0, k1 in ((0, nk - P), (nk - P, nk)):
                        out = acc[:, 2 * (u % 2) + i, k0:k1]
                        mm(out, z[rows, h, q0:q0 + P], z[rows, 8 + h, PAD + k0:PAD + k1], start=True, stop=(k0 == 0))
                    mm(out, ident[:], causal[:], start=False, stop=True).then_inc(pa_s, 1)

            def p_out(u):
                h, blk = u // 2, u % 2
                tiles = [(0, P), (P, P), (2 * P, N_META)] if blk else [(0, P), (P, N_META)]
                pe.wait_ge(pa_v, 4 * (u + 1))
                if u >= 2:
                    pe.wait_ge(pa_tc, 2 * (u - 1))
                for i, (k0, n) in enumerate(tiles):
                    last = transpose(aux[0:n, u % 2, P * i:P * (i + 1)], prob[:, 2 * (u % 2), k0:k0 + n], ident[:])
                last.then_inc(pa_t, 1)
                pe.wait_ge(pa_tc, 2 * (u + 1))
                if u >= 2:
                    pe.wait_ge(pa_oc, u - 1)
                for i, (k0, n) in enumerate(tiles):
                    last = mm(aux[:, 2 + u % 2, 0:P], v_nat[0:n, i, P * h:P * (h + 1)], probT[0:n, u % 2, i, :],
                              start=(i == 0), stop=(i == len(tiles) - 1))
                last.then_inc(pa_o, 1)

            p_score(0)
            for u in range(16):
                if u < 15:
                    p_score(u + 1)
                p_out(u)

            pe.wait_ge(nw_e, 1)
            pe.wait_ge(pa_oc, 16)
            mm(aux[:, 2, :], ones[0:N_SMP, :], s_new[:].rearrange("p s h c -> p (s h c)"),
               start=True, stop=True).then_inc(nw_m, 1)
            for h in range(N_H):
                last = mm(aux[:, 3, :].rearrange("p (s h c) -> p s h c", h=N_H, c=QC)[:, :, h, :],
                          v_nat[0:N_SMP, 3, P * h:P * (h + 1)], s_new[:, :, h, :], start=True, stop=True)
            last.then_inc(nw_m, 1)
            for h in range(N_H):
                pe.wait_ge(sub_sq, h + 1)
                if h >= 2:
                    pe.wait_ge(sub_rt, h - 1)
                mm(aux[:, h % 2, 0:T_OUT], ones[:], tmp[:, h % 2, 0:T_OUT], start=True, stop=True)\
                  .then_inc(sub_mm, 1)
            pe.wait_ge(cv_s, CV_S)
            pe.wait_ge(cv_p, 8 * TAPS)
            pe.wait_ge(nw_v, 4)
            for c in range(8):
                last = mm(aux[:, 2, 0:T_OUT], ones[:], z[:, 16 + c, 0:T_OUT], start=(c == 0), stop=(c == 7))
            last.then_inc(ln_mm, 1)
            for c in range(8):
                pe.wait_ge(ln_sq, c + 1)
                last = mm(aux[:, 3, 0:T_OUT], ones[:], tmp[:, 2 + c % 2, 0:T_OUT], start=(c == 0), stop=(c == 7))
                last.then_inc(ln_mm, 1)

            for kt in range(KT):
                pe.wait_ge(a_lo_ok, KT + kt + 1)
                products(OUT_V0, kt, a_hi, a_lo, 0, T_OUT)
            with pe.Fori(OUT_V0 + 1, MLP_V0) as n:
                for kt in range(KT):
                    products(n, kt, a_hi, a_lo, 0, T_OUT)
            for kt in range(KT):
                pe.wait_ge(x2_sq, kt + 1)
                last = mm(aux[:, 0, 0:T_OUT], ones[:], tmp[:, kt % 4, 0:T_OUT], start=(kt == 0),
                          stop=(kt == KT - 1))
                last.then_inc(x2_mm, 1)
            with pe.Fori(0, N_QTR) as q:
                with pe.Fori(0, UP_N) as u:
                    for kt in range(KT):
                        pe.wait_ge(a_lo_ok, 2 * KT + kt + 1)
                        products(MLP_V0 + q * QTR_N + u, kt, a_hi, a_lo, 0, T_OUT)
                with pe.Fori(0, DOWN_N) as d:
                    for kt in range(KT):
                        pe.wait_ge(h_lo_ok, KT * q + kt + 1)
                        products(MLP_V0 + UP_N + q * QTR_N + d, kt, h_hi, h_lo, 0, T_OUT)
            for g in range(4):
                pe.wait_ge(acc_free, MT + MT * (MLP_V0 + N_QTR * QTR_N - DOWN_N + g + 1))
                for i, (t0, n) in enumerate(((N_META, P), (N_META + P, P), (T_P, N_SMP))):
                    b = 3 * g + i
                    if b >= 4:
                        pe.wait_ge(y_a if b % 2 == 0 else y_d, (b - 4) // 2 + 1)
                    for m in range(MT):
                        last = transpose(aux[0:n, b % 4, P * m:P * (m + 1)], xT[:, MT * g + m, t0:t0 + n], ident[:])
                    last.then_inc(y_mm, 1)

        def free(eng, n, j):
            if j == 1:
                eng.wait_ge(acc_ok, MT * n)
            else:
                eng.wait_ge(w_used, (NC - 1) * n + max(j - 1, 0))

        @block.scalar
        def _(act):
            fn = nc.scalar.activation

            def hi(n, j):
                act.wait_ge(raw_in[j % RAW], 16 * (NC // RAW * n + j // RAW + 1))
                free(act, n, j)
                nc.scalar.copy(w_hi[:, j % SPL], raw[:, j % RAW]).then_inc(hi_ok, 1)

            def sqrt(out, in_, count):
                return fn(out, in_, ACT.Sqrt, scale=1.0 / count, bias=eps[0:out.shape[0], :])

            act.sem_inc(kT_ok[0], 1)
            act.wait_ge(consts, CONSTS)
            act.wait_ge(set_v, 1)
            for kt in range(KT):
                act.wait_ge(x_kept, kt + 1)
                fn(a_hi[:, kt, :], xT[:, kt, :], ACT.Copy, scale=vec[:, V_ATTN + kt:V_ATTN + kt + 1])\
                    .then_inc(a_hi_ok, 1)
                if kt == 7:
                    hi(0, 0)
            hi(0, 1)
            for t, (_, n) in enumerate(TOK):
                act.wait_ge(x_in[t], 16 if t == 1 else 32)
                fn(z[0:n, 7 * t:7 * t + 7, :].rearrange("p a b -> p (a b)")[:, 0:D], x_nat[0:n, t, :], ACT.Square,
                   accum_out=sums[0:n, t:t + 1]).then_inc(sq_x, 1)
            act.wait_ge(sq_x, 3)
            sqrt(root[:, 0:2], sums[:, 0:2], D).then_inc(sq_x, 1)
            sqrt(root[0:48, 2:3], sums[0:48, 2:3], D).then_inc(sq_x, 1)
            for j in range(2, NC):
                hi(0, j)
            hi(1, 0)
            with act.Fori(1, ATT_FIRST) as n:
                hi(n, 1)
                for m in range(MT):
                    act.wait_ge(acc_free, MT + MT * (n - 1) + m + 1)
                    act.wait_ge(nrm_v, 1 + 2 * MT * (n - 1))
                    fn(tmp[:, m, :], z[:, ds(MT * (n - 1) + m, 1), PAD:ZW].rearrange("p a t -> p (a t)"),
                       ACT.Square).then_inc(nrm_sq, 1)
                for j in range(2, 5):
                    hi(n, j)
                for m in range(MT):
                    act.wait_ge(nrm_sum, MT * (n - 1) + m + 1)
                    sqrt(tmp[:, m, :], aux[:, m, 0:T], HD).then_inc(nrm_root, 1)
                for j in range(5, NC):
                    hi(n, j)
                hi(n + 1, 0)

            def sequence(s, n):
                w_at = {0: 1, 5: 2, 10: 3, 15: 4}
                for j in range(N_PAGES):
                    act.wait_ge(kT_mm[0], N_PAGES * s + j + 1)
                    act.wait_ge(sc_mm, N_PAGES * s + j + 1)
                    nc.scalar.copy(kT[:, j % 2, 0:4, :], aux[:, 0, :].rearrange("p (h k) -> p h k", h=4))\
                        .then_inc(kT_ok[0], 1)
                    if n is not None and j in w_at:
                        hi(n, w_at[j])
                if n is not None:
                    hi(n, 5)
                for half in range(2):
                    act.wait_ge(sub_ok, 2 * s + half + 1)
                    sh = S[:, 8 * half:8 * half + 8, :]
                    fn(sh, sh, ACT.Exp).then_inc(exp_ok, 1)
                if n is not None:
                    hi(n, 6)
                    hi(n, 7)
                    hi(n + 1, 0)

            with act.Fori(0, Z_VISITS - ATT_FIRST) as s:
                sequence(s, s + ATT_FIRST)
            with act.Fori(Z_VISITS - ATT_FIRST, N_ATT_V) as s:
                sequence(s, s + ATT_FIRST)
                for m in range(MT):
                    act.wait_ge(acc_free, MT + MT * (s + ATT_FIRST) + m + 1)
                    fn(tmp[:, m, :], tmp[:, m, :], ACT.Exp, scale=-1.0).then_inc(gate_e, 1)
            b = 0
            for buf, parts in ((v_nat, NAT), (k_nat, NAT), (g_nat, ((0, 30), (0, N_SMP)))):
                if buf is k_nat:
                    with act.Fori(N_ATT_V, N_SEQ) as s:
                        sequence(s, None)
                for i, (_, n) in enumerate(parts):
                    act.wait_ge(nat_mm, b + 1)
                    nc.scalar.copy(buf[0:n, i, 0:512], acc[0:n, b % 4, :]).then_inc(nat_a, 1)
                    b += 2
            act.wait_ge(lam_v, 2)
            fn(lam_exp[:], lam_sum[:], ACT.Exp).then_inc(lam_a, 1)

            def p_exp(u):
                nk = N_META + P * (u % 2 + 1)
                for i in range(2):
                    act.wait_ge(pa_max, 2 * u + i + 1)
                    if u >= 2:
                        act.wait_ge(pa_t, u - 1)
                    fn(prob[:, 2 * (u % 2) + i, 0:nk], acc[:, 2 * (u % 2) + i, 0:nk], ACT.Exp,
                       bias=pstat[:, u % 2, i:i + 1], accum_out=pstat[:, u % 2, 2 + i:3 + i]).then_inc(pa_exp, 1)

            def p_copy(u):
                act.wait_ge(pa_t, u + 1)
                if u >= 2:
                    act.wait_ge(pa_o, u - 1)
                full = u % 2 + 1
                nc.scalar.copy(probT[:, u % 2, 0:full, :],
                               aux[:, u % 2, 0:P * full].rearrange("p (a q) -> p a q", q=P)).then_inc(pa_tc, 1)
                nc.scalar.copy(probT[0:N_META, u % 2, full, :], aux[0:N_META, u % 2, P * full:P * (full + 1)])\
                    .then_inc(pa_tc, 1)

            p_exp(0)
            for u in range(16):
                if u < 15:
                    p_exp(u + 1)
                p_copy(u)
            act.wait_ge(nw_v, 1)
            fn(s_new[:], s_new[:], ACT.Exp).then_inc(nw_e, 1)

            for h in range(N_H):
                if h == 0:
                    act.wait_ge(nw_v, 7)
                    act.wait_ge(pa_oc, 16)
                if h >= 2:
                    act.wait_ge(sub_v, 2 * (h - 1))
                fn(tmp[:, h % 2, 0:T_OUT], z[:, h, PAD + N_META:ZW], ACT.Square).then_inc(sub_sq, 1)
                act.wait_ge(sub_mm, h + 1)
                sqrt(tmp[:, h % 2, 0:T_OUT], aux[:, h % 2, 0:T_OUT], P).then_inc(sub_rt, 1)
                act.wait_ge(sub_v, 2 * (h + 1))
                if h == 0:
                    act.wait_ge(v_out, 16 * 4)
                nc.scalar.copy(a_hi[:, h, 0:T_OUT], z[:, h, PAD + N_META:ZW]).then_inc(a_hi_ok, 1)
            for c in range(8):
                act.wait_ge(ln_v, c + 1)
                if c >= 2:
                    act.wait_ge(ln_mm, c)
                fn(tmp[:, 2 + c % 2, 0:T_OUT], z[:, 16 + c, 0:T_OUT], ACT.Square).then_inc(ln_sq, 1)
            act.wait_ge(ln_mm, 9)
            sqrt(rstd[:, 0:T_OUT], aux[:, 3, 0:T_OUT], D_CONV).then_inc(ln_rt, 1)
            for c in range(8):
                act.wait_ge(ln_n, 1 + 2 * (c + 1))
                if c >= 4:
                    act.wait_ge(ln_s, 3 * (c - 3))
                fn(tmp[:, c % 4, 0:T_OUT], z[:, 16 + c, 0:T_OUT], ACT.Exp, scale=-1.0).then_inc(ln_e, 1)
                act.wait_ge(ln_s, 3 * (c + 1))
                nc.scalar.copy(a_hi[:, 8 + c, 0:T_OUT], z[:, 16 + c, 0:T_OUT]).then_inc(a_hi_ok, 1)

            with act.Fori(OUT_V0, MLP_V0) as n:
                for j in range(1, NC):
                    hi(n, j)
                hi(n + 1, 0)
            for kt in range(KT):
                act.wait_ge(acc_free, MT + MT * (OUT_V0 + kt // 4) + kt % 4 + 1)
                if kt >= 4:
                    act.wait_ge(x2_mm, kt - 3)
                fn(tmp[:, kt % 4, 0:T_OUT], xT[:, kt, N_META:T], ACT.Square).then_inc(x2_sq, 1)
                if kt == 0:
                    act.wait_ge(acc_ok, MT * MLP_V0)
                fn(a_hi[:, kt, 0:T_OUT], xT[:, kt, N_META:T], ACT.Copy, scale=vec[:, V_MLP + kt:V_MLP + kt + 1])\
                    .then_inc(a_hi_ok, 1)
            act.wait_ge(x2_mm, KT)
            sqrt(rstd[:, 0:T_OUT], aux[:, 0, 0:T_OUT], D).then_inc(x2_rt, 1)

            def up(n, q, u):
                for j in range(1, NC):
                    hi(n, j)
                hi(n + 1, 0)
                for m in range(MT):
                    i = KT * q + MT * u + m
                    act.wait_ge(acc_free, MT + MT * n + m + 1)
                    fn(tmp[:, m, 0:T_OUT], tmp[:, m, 0:T_OUT], ACT.Square).then_inc(up_h, 1)
                    act.wait_ge(up_h, i + 1)
                    nc.scalar.copy(h_hi[:, ds(MT * u + m, 1), :].rearrange("p a t -> p (a t)"),
                                   tmp[:, m, 0:T_OUT]).then_inc(h_hi_ok, 1)

            def down(n, last=False):
                for j in range(1, NC):
                    hi(n, j)
                if not last:
                    hi(n + 1, 0)

            with act.Fori(0, N_QTR - 1) as q:
                with act.Fori(0, UP_N) as u:
                    up(MLP_V0 + q * QTR_N + u, q, u)
                with act.Fori(0, DOWN_N) as d:
                    down(MLP_V0 + UP_N + q * QTR_N + d)
            n0 = MLP_V0 + (N_QTR - 1) * QTR_N
            with act.Fori(0, UP_N) as u:
                up(n0 + u, N_QTR - 1, u)
            with act.Fori(0, DOWN_N - 1) as d:
                down(n0 + UP_N + d)
            down(n0 + UP_N + DOWN_N - 1, last=True)
            for b in range(0, 12, 2):
                g, i = b // 3, b % 3
                n = P if i < 2 else N_SMP
                dst = y_nat[:, i, VC * g:VC * (g + 1)] if i < 2 else y_smp[:, VC * g:VC * (g + 1)]
                act.wait_ge(y_mm, b + 1)
                if b == 0:
                    act.wait_ge(kc_out, 16 * KC_STORES)
                nc.scalar.copy(dst, aux[0:n, b % 4, :]).then_inc(y_a, 1)

        @block.vector
        def _(dve):
            v = nc.vector
            dve.sem_inc(lo_ok, RAW)
            dve.sem_inc(acc_free, MT)
            dve.sem_inc(kT_ok[1], 1)
            dve.sem_inc(o_ok, 1)
            dve.sem_inc(l_ok, 1)
            dve.sem_inc(nrm_v, 1)

            def lo(n, j):
                dve.wait_ge(hi_ok, NC * n + j + 1)
                free(dve, n, j)
                v.tensor_tensor(w_lo[:, j % SPL], raw[:, j % RAW], w_hi[:, j % SPL].bitcast(F32), ALU.subtract)\
                    .then_inc(lo_ok, 1)

            def take(n, dst, plain=None):
                for m in range(MT):
                    dve.wait_ge(acc_ok, MT * n + m + 1)
                    v.tensor_tensor(dst(m), acc[:, m, 0:T], rstd[:], ALU.mult).then_inc(acc_free, 1)

            def z_tile(i):
                return z[:, ds(i, 1), PAD:ZW].rearrange("p a t -> p (a t)")

            dve.wait_ge(set_t, 1)
            v.tensor_copy(vec[:], aux[:, 0, 0:N_VEC]).then_inc(set_v, 1)
            for kt in range(KT):
                dve.wait_ge(x_turned, kt + 1)
                v.tensor_copy(xT[:, kt, :], acc[:, kt % 4, 0:T]).then_inc(x_kept, 1)
                if kt >= 1:
                    k = kt - 1
                    dve.wait_ge(a_hi_ok, k + 1)
                    v.scalar_tensor_tensor(a_lo[:, k, :], xT[:, k, :], vec[:, V_ATTN + k:V_ATTN + k + 1],
                                           a_hi[:, k, :].bitcast(F32), ALU.mult, ALU.subtract).then_inc(a_lo_ok, 1)
                if kt == 9:
                    lo(0, 0)
            dve.wait_ge(a_hi_ok, KT)
            k = KT - 1
            v.scalar_tensor_tensor(a_lo[:, k, :], xT[:, k, :], vec[:, V_ATTN + k:V_ATTN + k + 1],
                                   a_hi[:, k, :].bitcast(F32), ALU.mult, ALU.subtract).then_inc(a_lo_ok, 1)
            lo(0, 1)
            v.memset(z[:, 24:32, 0:PAD], 0.0)
            v.tensor_scalar(vec[:, V_SUB:V_SUB + 1], vec[:, V_SUB:V_SUB + 1], 1.0 - LAMBDA_INIT, None, ALU.mult)\
                .then_inc(set_v, 1)
            v.tensor_scalar(qk_gain[:, 0:8], ones[:, 0:8], vec[:, V_Q:V_Q + 1], HD ** -0.5, ALU.mult, ALU.mult)\
                .then_inc(set_v, 1)
            v.tensor_scalar(qk_gain[:, 8:16], ones[:, 0:8], vec[:, V_K:V_K + 1], None, ALU.mult).then_inc(set_v, 1)
            dve.wait_ge(set_t, 2)
            v.tensor_copy(taps[:], aux[:, 1, 0:8 * TAPS].rearrange("p (c t) -> p c t", t=TAPS)).then_inc(set_v, 1)
            for g in range(4):
                dve.wait_ge(set_t, 3 + g)
                c0, s0 = 4 * (g % 2), 4 * (g // 2)
                v.tensor_copy(ext[:, c0:c0 + 4, s0:s0 + 4, 0:TAPS - 1],
                              aux[:, (2, 3, 1, 2)[g], 0:480].rearrange("p (c s t) -> p c s t", c=4, s=4))\
                    .then_inc(set_v, 1)
            lo(0, 2)
            dve.wait_ge(sq_x, 5)
            v.reciprocal(inv[:, 0:2], root[:, 0:2]).then_inc(set_v, 1)
            v.reciprocal(inv[0:48, 2:3], root[0:48, 2:3]).then_inc(set_v, 1)
            dve.wait_ge(set_v, 11)
            for t, (_, n) in enumerate(TOK):
                v.tensor_scalar(rb[0:n, t, :], ones[0:n, :], inv[0:n, t:t + 1], None, ALU.mult).then_inc(set_v, 1)
            for j in range(3, 6):
                lo(0, j)
            dve.wait_ge(set_t, 7)
            v.tensor_copy(rstd[:], aux[:, 0, 0:T]).then_inc(set_v, 1)
            dve.wait_ge(set_v, 15)
            for j in range(6, NC):
                lo(0, j)
            lo(1, 0)
            take(0, z_tile)
            with dve.Fori(1, ATT_FIRST) as n:
                for j in range(1, 6):
                    lo(n, j)
                done = 1 + 2 * MT * (n - 1)
                for m in range(MT):
                    dve.wait_ge(nrm_root, MT * (n - 1) + m + 1)
                    v.reciprocal(tmp[:, m, :], tmp[:, m, :]).then_inc(nrm_v, 1)
                for m in range(MT):
                    dve.wait_ge(nrm_v, done + m + 1)
                    i = MT * (n - 1) + m
                    v.scalar_tensor_tensor(z_tile(i), z_tile(i), qk_gain[:, ds(i, 1)], tmp[:, m, :],
                                           ALU.mult, ALU.mult).then_inc(nrm_v, 1)
                for j in range(6, NC):
                    lo(n, j)
                lo(n + 1, 0)
                take(n, lambda m: z_tile(MT * n + m))
            dve.wait_ge(nrm_v, 1 + 2 * MT * NORM_VISITS)
            for i in range(2):
                rows = slice(HD * i, HD * (i + 1))
                v.tensor_copy(q_new[rows, :, :, DEC * i:DEC * (i + 1)],
                              z[rows, 0:8, PAD + T_P:ZW].rearrange("p h (s t) -> p s h t", t=DEC)).then_inc(q_ok, 1)
            dve.wait_ge(sn_mm, 1)
            v.tensor_tensor(s_new[:].rearrange("p s h (i t) -> p s (h i) t", t=DEC),
                            aux[0:N_SMP, 0, :].rearrange("p (s g t) -> p s g t", s=N_SEQ, t=DEC),
                            new_mask[:].unsqueeze(2).to_broadcast([N_SMP, N_SEQ, 2 * N_H, DEC]), ALU.add)\
                .then_inc(sn_ok, 1)

            def conv_tap(base, i, ch, j):
                def tile(t, c0):
                    return z[:, ds(t, 1), c0:c0 + SEQ].rearrange("p a t -> p (a t)")
                src, dst = tile(24 + ch, 2 + j), tile(16 + ch, 0)
                w = taps[:, ds(ch, 1), j:j + 1].rearrange("p a t -> p (a t)")
                if j == 0:
                    v.tensor_scalar(dst, src, w, vec[:, ds(V_DWB + ch, 1)], ALU.mult, ALU.add).then_inc(cv_p, 1)
                else:
                    v.scalar_tensor_tensor(dst, src, w, dst, ALU.mult, ALU.add).then_inc(cv_p, 1)

            def sequence(s, n, chs=()):
                k = len(chs)
                work = iter([(i, j, c) for i, (j, c) in enumerate((j, c) for j in range(TAPS) for c in range(k))])
                base = 3 * TAPS * (s - N_ATT_V) if k else None

                def conv(count):
                    for _ in range(count):
                        item = next(work, None)
                        if item:
                            i, j, c = item
                            if i >= k:
                                dve.wait_ge(cv_p, base + i - k + 1)
                            conv_tap(base, i, chs[c], j)
                w_at = {0: 1, 5: 2, 10: 3, 15: 4}
                for j in range(N_PAGES):
                    dve.wait_ge(kT_mm[1], N_PAGES * s + j + 1)
                    dve.wait_ge(sc_mm, N_PAGES * s + j + 1)
                    v.tensor_copy(kT[:, j % 2, 4:8, :], aux[:, 1, :].rearrange("p (h k) -> p h k", h=4))\
                        .then_inc(kT_ok[1], 1)
                    if n is not None and j in w_at:
                        lo(n, w_at[j])
                    if j >= 1:
                        dve.wait_ge(sc_mm, 2 + N_PAGES * s + j)
                        v.tensor_copy(S[:, j - 1, :], aux[:, 2, 0:SC]).then_inc(sc_ok, 1)
                    conv(3)
                dve.wait_ge(sc_mm, 2 + N_PAGES * s + N_PAGES)
                v.tensor_copy(S[:, N_PAGES - 1, :], aux[:, 2, 0:SC]).then_inc(sc_ok, 1)
                dve.wait_ge(sc_ok, N_PAGES * (s + 1))
                v.tensor_reduce(pmax[:, 0:SC], S[:].rearrange("p j c -> p c j"), AX, ALU.max).then_inc(mx_v, 1)
                dve.wait_ge(mx_v, 4 * s + 1)
                v.tensor_tensor(pmax[0:N_SMP, 0:SC], pmax[0:N_SMP, 0:SC],
                                s_new[:, ds(s, 1)].rearrange("p a h c -> p (a h c)"), ALU.max).then_inc(mx_v, 1)
                dve.wait_ge(mx_mm, 2 * s + 1)
                v.tensor_reduce(nm[:], aux[0:SC, 2, P:2 * P], AX, ALU.max, negate=True).then_inc(mx_v, 1)
                dve.wait_ge(mx_v, 4 * s + 3)
                v.tensor_scalar(nm_diag[:], ident[0:SC, 0:SC], nm[:, 0:1], None, ALU.mult).then_inc(mx_v, 1)
                dve.wait_ge(mx_mm, 2 * s + 2)
                nmax = neg_max[:, ds(s, 1), :]
                v.tensor_copy(nmax.rearrange("p a c -> p (a c)"), aux[:, 2, 2 * P:2 * P + SC]).then_inc(nm_ok, 1)
                dve.wait_ge(nm_ok, s + 1)
                for half in range(2):
                    sh = S[:, 8 * half:8 * half + 8, :]
                    v.tensor_tensor(sh, sh, nmax.to_broadcast([P, 8, SC]), ALU.add).then_inc(sub_ok, 1)
                if n is not None:
                    lo(n, 5)
                    lo(n, 6)
                dve.wait_ge(exp_ok, 2 * s + 2)
                v.tensor_reduce(lpart[:], S[:].rearrange("p j c -> p c j"), AX, ALU.add).then_inc(lp_ok, 1)
                if n is not None:
                    lo(n, 7)
                    lo(n + 1, 0)
                conv(3 * TAPS)
                dve.wait_ge(pv_mm, N_PAGES * (s + 1))
                v.tensor_copy(o_cache[:, ds(s, 1), :].rearrange("p a c -> p (a c)"), aux[:, 3, 0:SC]).then_inc(o_ok, 1)
                dve.wait_ge(l_mm, s + 1)
                v.tensor_copy(l_cache[:, ds(s, 1), :].rearrange("p a c -> p (a c)"), aux[:, 2, 3 * P:3 * P + SC])\
                    .then_inc(l_ok, 1)

            with dve.Fori(0, Z_VISITS - ATT_FIRST) as s:
                sequence(s, s + ATT_FIRST)
                take(s + ATT_FIRST, lambda m: z_tile(MT * (s + ATT_FIRST) + m))
            with dve.Fori(Z_VISITS - ATT_FIRST, N_ATT_V) as s:
                n = s + ATT_FIRST
                sequence(s, n)
                take(n, lambda m: tmp[:, m, :])
                g0 = 3 * MT * (n - Z_VISITS)
                for m in range(MT):
                    dve.wait_ge(gate_e, MT * (n - Z_VISITS) + m + 1)
                    v.tensor_scalar(tmp[:, m, :], tmp[:, m, :], 1.0, None, ALU.add).then_inc(gate_v, 1)
                for m in range(MT):
                    dve.wait_ge(gate_v, g0 + m + 1)
                    v.reciprocal(tmp[:, m, :], tmp[:, m, :]).then_inc(gate_v, 1)
                for m in range(MT):
                    dve.wait_ge(gate_v, g0 + MT + m + 1)
                    t = z_tile(24 + MT * (n - Z_VISITS) + m)
                    v.tensor_tensor(t, t, tmp[:, m, :], ALU.mult).then_inc(gate_v, 1)

            b = 0
            for buf, parts in ((v_nat, NAT), (k_nat, NAT), (g_nat, ((0, 30), (0, N_SMP)))):
                if buf is k_nat:
                    dve.wait_ge(nat_mm, 8)
                    with dve.Fori(N_ATT_V, N_SEQ - 1) as s:
                        sequence(s, None, [3 * (s - N_ATT_V) + c for c in range(3)])
                    sequence(N_SEQ - 1, None, [6, 7])
                for i, (_, n) in enumerate(parts):
                    dve.wait_ge(nat_mm, b + 2)
                    v.tensor_copy(buf[0:n, i, 512:1024], acc[0:n, (b + 1) % 4, :]).then_inc(nat_d, 1)
                    b += 2
            dve.wait_ge(state_in, STATE)
            v.tensor_tensor(lam_prod[:], lam_in[:, 0:2, :], lam_in[:, 2:4, :], ALU.mult).then_inc(lam_v, 1)
            dve.wait_ge(lam_v, 1)
            v.tensor_reduce(lam_sum[:], lam_prod[:], AX, ALU.add).then_inc(lam_v, 1)
            dve.wait_ge(lam_a, 1)
            v.tensor_tensor(lam_one[:], lam_exp[:, 0:1], lam_exp[:, 1:2], ALU.subtract).then_inc(lam_v, 1)
            dve.wait_ge(lam_v, 3)
            v.tensor_scalar(lam_one[:], lam_one[:], LAMBDA_INIT, None, ALU.add).then_inc(lam_v, 1)
            dve.wait_ge(lam_m, 1)
            v.tensor_scalar(neg_lam[:], aux[:, 2, 0:1], -1.0, None, ALU.mult).then_inc(lam_v, 1)
            dve.wait_ge(lam_v, 5)

            def p_max(u):
                nk = N_META + P * (u % 2 + 1)
                for i in range(2):
                    dve.wait_ge(pa_s, 2 * u + i + 1)
                    v.tensor_reduce(pstat[:, u % 2, i:i + 1], acc[:, 2 * (u % 2) + i, 0:nk], AX, ALU.max,
                                    negate=True).then_inc(pa_max, 1)

            def p_diff(u):
                nk = N_META + P * (u % 2 + 1)
                st, p1, p2 = pstat[:, u % 2, :], prob[:, 2 * (u % 2), 0:nk], prob[:, 2 * (u % 2) + 1, 0:nk]
                dve.wait_ge(pa_exp, 2 * (u + 1))
                v.reciprocal(st[:, 2:4], st[:, 2:4]).then_inc(pa_v, 1)
                dve.wait_ge(pa_v, 4 * u + 1)
                v.tensor_tensor(st[:, 3:4], st[:, 3:4], neg_lam[:], ALU.mult).then_inc(pa_v, 1)
                v.tensor_scalar(p1, p1, st[:, 2:3], None, ALU.mult).then_inc(pa_v, 1)
                dve.wait_ge(pa_v, 4 * u + 3)
                v.scalar_tensor_tensor(p1, p2, st[:, 3:4], p1, ALU.mult, ALU.add).then_inc(pa_v, 1)

            def p_take(u):
                h, blk = u // 2, u % 2
                c0 = PAD + N_META + P * blk
                dve.wait_ge(pa_o, u + 1)
                v.tensor_copy(z[:, h, c0:c0 + P], aux[:, 2 + u % 2, 0:P]).then_inc(pa_oc, 1)

            p_max(0)
            for u in range(16):
                if u < 15:
                    p_max(u + 1)
                p_diff(u)
                if u >= 1:
                    p_take(u - 1)
            p_take(15)

            flat = lambda t: t[:].rearrange("p s c -> p (s c)")
            dve.wait_ge(nm_ok, N_SEQ)
            s_flat = s_new[:].rearrange("p s h c -> p (s h c)")
            v.tensor_tensor(s_flat, s_flat, flat(neg_max)[0:N_SMP, :], ALU.add).then_inc(nw_v, 1)
            dve.wait_ge(nw_m, 2)
            v.tensor_tensor(flat(l_cache), flat(l_cache), aux[:, 2, :], ALU.add).then_inc(nw_v, 1)
            dve.wait_ge(nw_v, 2)
            v.reciprocal(flat(l_cache), flat(l_cache)).then_inc(nw_v, 1)
            v.tensor_tensor(flat(o_cache), flat(o_cache), aux[:, 3, :], ALU.add).then_inc(nw_v, 1)
            dve.wait_ge(nw_v, 4)
            v.tensor_tensor(flat(o_cache), flat(o_cache), flat(l_cache), ALU.mult).then_inc(nw_v, 1)
            dve.wait_ge(nw_v, 5)
            o4 = o_cache[:].rearrange("p s (h i t) -> p (s h) i t", i=2, t=DEC)
            v.scalar_tensor_tensor(o_smp[:], o4[:, :, 1, :], neg_lam[:, 0:1], o4[:, :, 0, :],
                                   ALU.mult, ALU.add).then_inc(nw_v, 1)
            dve.wait_ge(nw_v, 6)
            v.tensor_copy(z[:, 0:8, PAD + T_P:ZW].rearrange("p h (s t) -> p s h t", t=DEC),
                          o_smp[:].rearrange("p (s h) t -> p s h t", h=N_H)).then_inc(nw_v, 1)

            def rest(i, src):
                dve.wait_ge(a_hi_ok, KT + i + 1)
                v.tensor_tensor(a_lo[:, i, 0:T_OUT], src, a_hi[:, i, 0:T_OUT].bitcast(F32), ALU.subtract)\
                    .then_inc(a_lo_ok, 1)

            for h in range(N_H):
                o = z[:, h, PAD + N_META:ZW]
                dve.wait_ge(sub_rt, h + 1)
                r = tmp[:, h % 2, 0:T_OUT]
                v.reciprocal(r, r).then_inc(sub_v, 1)
                dve.wait_ge(sub_v, 2 * h + 1)
                v.scalar_tensor_tensor(o, o, vec[:, V_SUB:V_SUB + 1], r, ALU.mult, ALU.mult).then_inc(sub_v, 1)
                rest(h, o)
            conv_t = [z[:, 16 + c, 0:T_OUT] for c in range(8)]
            dve.wait_ge(ln_mm, 1)
            for c in range(8):
                v.scalar_tensor_tensor(conv_t[c], aux[:, 2, 0:T_OUT], -1.0 / D_CONV, conv_t[c],
                                       ALU.mult, ALU.add).then_inc(ln_v, 1)
            dve.wait_ge(ln_rt, 1)
            v.reciprocal(rstd[:, 0:T_OUT], rstd[:, 0:T_OUT]).then_inc(ln_n, 1)
            dve.wait_ge(ln_n, 1)
            for c in range(8):
                v.scalar_tensor_tensor(conv_t[c], conv_t[c], vec[:, V_LNG + c:V_LNG + c + 1], rstd[:, 0:T_OUT],
                                       ALU.mult, ALU.mult).then_inc(ln_n, 1)
                dve.wait_ge(ln_n, 1 + 2 * c + 1)
                v.tensor_scalar(conv_t[c], conv_t[c], vec[:, V_LNB + c:V_LNB + c + 1], None, ALU.add)\
                    .then_inc(ln_n, 1)
            for c in range(8):
                e = tmp[:, c % 4, 0:T_OUT]
                dve.wait_ge(ln_e, c + 1)
                v.tensor_scalar(e, e, 1.0, None, ALU.add).then_inc(ln_s, 1)
                dve.wait_ge(ln_s, 3 * c + 1)
                v.reciprocal(e, e).then_inc(ln_s, 1)
                dve.wait_ge(ln_s, 3 * c + 2)
                v.tensor_tensor(conv_t[c], conv_t[c], e, ALU.mult).then_inc(ln_s, 1)
                rest(8 + c, conv_t[c])

            def add_x(n, i0):
                for m in range(MT):
                    x = xT[:, ds(i0 + m, 1), N_META:T].rearrange("p a t -> p (a t)")
                    dve.wait_ge(acc_ok, MT * n + m + 1)
                    v.tensor_tensor(x, x, acc[:, m, 0:T_OUT], ALU.add).then_inc(acc_free, 1)

            with dve.Fori(OUT_V0, MLP_V0) as n:
                for j in range(1, NC):
                    lo(n, j)
                lo(n + 1, 0)
                add_x(n, MT * (n - OUT_V0))
            for kt in range(KT):
                dve.wait_ge(a_hi_ok, 2 * KT + kt + 1)
                v.scalar_tensor_tensor(a_lo[:, kt, 0:T_OUT], xT[:, kt, N_META:T], vec[:, V_MLP + kt:V_MLP + kt + 1],
                                       a_hi[:, kt, 0:T_OUT].bitcast(F32), ALU.mult, ALU.subtract)\
                    .then_inc(a_lo_ok, 1)
            dve.wait_ge(x2_rt, 1)
            v.reciprocal(rstd[:, 0:T_OUT], rstd[:, 0:T_OUT]).then_inc(x2_v, 1)
            dve.wait_ge(x2_v, 1)

            def up(n, q, u):
                for j in range(1, NC):
                    lo(n, j)
                lo(n + 1, 0)
                for m in range(MT):
                    dve.wait_ge(acc_ok, MT * n + m + 1)
                    v.scalar_tensor_tensor(tmp[:, m, 0:T_OUT], acc[:, m, 0:T_OUT], 0.0, rstd[:, 0:T_OUT],
                                           ALU.max, ALU.mult).then_inc(acc_free, 1)
                for m in range(MT):
                    dve.wait_ge(h_hi_ok, KT * q + MT * u + m + 1)
                    t = lambda h: h[:, ds(MT * u + m, 1), :].rearrange("p a t -> p (a t)")
                    v.tensor_tensor(t(h_lo), tmp[:, m, 0:T_OUT], t(h_hi).bitcast(F32), ALU.subtract)\
                        .then_inc(h_lo_ok, 1)

            def down(n, d, last=False):
                for j in range(1, NC):
                    lo(n, j)
                if not last:
                    lo(n + 1, 0)
                add_x(n, MT * d)

            with dve.Fori(0, N_QTR - 1) as q:
                with dve.Fori(0, UP_N) as u:
                    up(MLP_V0 + q * QTR_N + u, q, u)
                with dve.Fori(0, DOWN_N) as d:
                    down(MLP_V0 + UP_N + q * QTR_N + d, d)
            n0 = MLP_V0 + (N_QTR - 1) * QTR_N
            with dve.Fori(0, UP_N) as u:
                up(n0 + u, N_QTR - 1, u)
            with dve.Fori(0, DOWN_N - 1) as d:
                down(n0 + UP_N + d, d)
            down(n0 + UP_N + DOWN_N - 1, DOWN_N - 1, last=True)
            dve.wait_ge(kc_out, 16 * KC_STORES)
            for b in range(1, 12, 2):
                g, i = b // 3, b % 3
                n = P if i < 2 else N_SMP
                dst = y_nat[:, i, VC * g:VC * (g + 1)] if i < 2 else y_smp[:, VC * g:VC * (g + 1)]
                dve.wait_ge(y_mm, b + 1)
                v.tensor_copy(dst, aux[0:n, b % 4, :]).then_inc(y_d, 1)


_INS = ["x_prompt", "x_sample", "cache_k", "cache_v", "state_conv", "page_table", "meta_tokens", "attn_norm",
        "w_in", "q_norm", "k_norm", "lambda_q1", "lambda_k1", "lambda_q2", "lambda_k2", "attn_subln", "dw_w",
        "dw_b", "conv_ln_g", "conv_ln_b", "w_out", "mlp_norm", "w_up", "w_down"]
_OUTS = [(1, SEQ, D), (N_SEQ, DEC, D), (1, 1, T_P, 2 * N_H, HD), (1, 1, T_P, N_H, 2 * HD),
         (1, 1, TAPS - 1, D_CONV), (1, N_SEQ, DEC, 2 * N_H, HD), (1, N_SEQ, DEC, N_H, 2 * HD),
         (1, N_SEQ, TAPS - 1, D_CONV)]


def kernel(**inputs):
    import numpy as _np
    import concourse.bacc as _bacc
    from concourse.bass_utils import run_bass_kernel_spmd as _run

    nc = _bacc.Bacc("TRN2", target_bir_lowering=False, num_devices=1)
    arrays, args = {}, []
    for name in _INS:
        a = _np.ascontiguousarray(inputs[name])
        arrays[f"in_{name}"] = a
        args.append(nc.dram_tensor(f"in_{name}", a.shape, mybir.dt.from_np(a.dtype), kind="ExternalInput").ap())
    for i, shape in enumerate(_OUTS):
        args.append(nc.dram_tensor(f"out_{i}", shape, F32, kind="ExternalOutput").ap())
    build_step(nc, *args)
    r = _run(nc, [arrays], core_ids=[0])
    return tuple(r.results[0][f"out_{i}"] for i in range(len(_OUTS)))
```

```python
from contextlib import ExitStack

import concourse.bass as bass
import concourse.mybir as mybir

F32 = mybir.dt.float32
F32R = mybir.dt.float32r
I32 = mybir.dt.int32
ALU = mybir.AluOpType
ACT = mybir.ActivationFunctionType
AX = mybir.AxisListType.X
ds = bass.ds

P = 128
EPS = 1e-6
NEG_INF = -1e30
LAMBDA_INIT = 0.2
N_META = 16
SEQ = 256
N_SEQ = 8
DEC = 4
N_SMP = N_SEQ * DEC
T_P = N_META + SEQ
T = T_P + N_SMP
T_OUT = T - N_META
D = 2048
KT = D // P
N_H = 8
HD = 64
D_ATTN = 1024
D_CONV = 1024
TAPS = 31
D_FF = 8192
D_IN = 3 * D_ATTN + 2 * D_CONV
N_PAGES = 16
VC = 512
MT = VC // P
CK = 2
NC = KT // CK
RAW = 4
SPL = 2
KR = 4
PG = 2 * KR
PAD = 16
ZW = PAD + T
QC = 2 * DEC
SC = N_H * QC
PAST = N_PAGES * P
SG = 4
NG = N_PAGES // SG
Q_V = D_IN // VC
Z_VISITS = 8
NORM_VISITS = 4
ATT_FIRST = 5
PAIR_V = Q_V - ATT_FIRST - 1
HB = 4
ATT_S = PAIR_V
CONV_S = 4
OUT_V0 = Q_V
OUT_N = D // VC
MLP_V0 = OUT_V0 + OUT_N
N_QTR = 4
FQ = D_FF // N_QTR
UP_N = FQ // VC
DOWN_N = D // VC
QTR_N = UP_N + DOWN_N
V_ATTN, V_MLP, V_DWB, V_LNG, V_LNB, V_SUB, V_Q, V_K = 0, 16, 32, 40, 48, 56, 57, 58
N_VEC = 59
KC_STORES = 4 + 1 + 2 * N_SEQ
CONSTS = 13
STATE = 16 * (N_SEQ + 1 + 4)
CV_S = 2 + 2 * TAPS
TOK = [(0, 128), (128, 128), (256, 48)]
NAT = [(0, 128), (128, 128), (256, 16), (T_P, N_SMP)]


def build_step(nc, x_prompt, x_sample, cache_k, cache_v, state_conv, page_table, meta_tokens,
               attn_norm, w_in, q_norm, k_norm, lambda_q1, lambda_k1, lambda_q2, lambda_k2,
               attn_subln, dw_w, dw_b, conv_ln_g, conv_ln_b, w_out, mlp_norm, w_up, w_down,
               y_prompt, y_sample, k_prompt, v_prompt, conv_prompt, k_sample, v_sample, conv_sample):
    ctx = ExitStack()
    with ctx:
        def sb(name, shape, dt=F32):
            return ctx.enter_context(nc.sbuf_tensor(name, shape, dt))

        def aliased(*layouts):
            made = []
            for group in layouts[:-1]:
                with ExitStack() as part:
                    made.append([part.enter_context(nc.sbuf_tensor(*g)) for g in group])
            made.append([sb(*g) for g in layouts[-1]])
            return made

        def sem(name):
            return ctx.enter_context(nc.semaphore(name))

        ident = sb("ident", [P, P])
        ones = sb("ones", [P, P])
        new_mask = sb("new_mask", [N_SMP, N_SEQ, DEC])
        eps = sb("eps", [P, 1])
        vec = sb("vec", [P, N_VEC])
        qk_gain = sb("qk_gain", [P, 16])
        taps = sb("taps", [P, 8, TAPS])
        neg_lam = sb("neg_lam", [P, 1])
        lam_sum = sb("lam_sum", [1, 2])
        lam_exp = sb("lam_exp", [1, 2])
        lam_one = sb("lam_one", [1, 1])
        pages_sb = sb("pages_sb", [1, N_SEQ * N_PAGES], I32)
        xT = sb("xT", [P, KT, T])
        rstd = sb("rstd", [P, T])
        sums = sb("sums", [P, 3])
        root = sb("root", [P, 3])
        inv = sb("inv", [P, 3])
        tmp = sb("tmp", [P, MT, T])
        raw = sb("raw", [P, RAW, CK, VC])
        w_hi = sb("w_hi", [P, SPL, CK, VC], F32R)
        w_lo = sb("w_lo", [P, SPL, CK, VC], F32R)
        (v_nat, k_nat, prob, probT, causal), (a_hi, a_lo) = aliased(
            [("v_nat", [P, 4, D_ATTN], F32), ("k_nat", [P, 4, D_ATTN], F32), ("prob", [P, 2, T_P], F32),
             ("probT", [P, 3, P], F32), ("causal", [P, P], F32)],
            [("a_hi", [P, KT, T], F32R), ("a_lo", [P, KT, T], F32R)])
        (h_hi, h_lo), (z,) = aliased(
            [("h_hi", [P, KT, T_OUT], F32R), ("h_lo", [P, KT, T_OUT], F32R)],
            [("z", [P, 32, ZW], F32)])
        (x_nat, st_nat), (y_nat, y_smp), (page,) = aliased(
            [("x_nat", [P, 3, D], F32), ("st_nat", [120, 2, D_CONV], F32)],
            [("y_nat", [P, 2, D], F32), ("y_smp", [N_SMP, D], F32)],
            [("page", [P, PG, D_ATTN], F32)])
        (cw_nat, vec_nat, head_ones, rb, lam_in, lam_prod), (kT,) = aliased(
            [("cw_nat", [TAPS, D_CONV], F32), ("vec_nat", [N_VEC, P], F32), ("head_ones", [P, P], F32),
             ("rb", [P, 3, P], F32), ("lam_in", [1, 4, HD], F32), ("lam_prod", [1, 2, HD], F32)],
            [("kT", [P, 2, N_H, P], F32)])
        pT = sb("pT", [P, N_PAGES, SC])
        s_rows = sb("s_rows", [SC, PAST + N_SMP])
        s_max = sb("s_max", [SC, NG + 1])
        s_sum = sb("s_sum", [SC, NG + 1])
        neg_max = sb("neg_max", [SC, 1])
        l_inv = sb("l_inv", [SC, 2])
        pick = sb("pick", [SC, 2, N_H, DEC])
        pick_s = sb("pick_s", [SC, 2, 4, DEC])
        q_cur = sb("q_cur", [P, N_H * (SC + QC)])
        s_cur = sb("s_cur", [N_SMP, SC])
        o_rows = sb("o_rows", [SC, 4 * P])
        s_new = sb("s_new", [N_SMP, N_SEQ, N_H, QC])
        o_cache = sb("o_cache", [P, N_SEQ, N_H * DEC])
        a_new = s_new[:].rearrange("p s (a h) c -> p s a (h c)", a=2)[:, :, 0, :]
        ext = sb("ext", [P, 8, N_SEQ, TAPS - 1 + DEC])
        c_smp = z[:, 16:24, SEQ:T_OUT].rearrange("p c (s t) -> p c s t", t=DEC)
        c_prod = sb("c_prod", [P, 8, N_SEQ, DEC])
        pstat = sb("pstat", [P, 4])
        flat_tmp = tmp[:].rearrange("p a t -> p (a t)")
        q_st = flat_tmp[:, 0:2 * SEQ].rearrange("p (i t) -> p i t", i=2)
        v_st = flat_tmp[:, 2 * SEQ:2 * SEQ + 3 * P].rearrange("p (i d) -> p i d", d=P)
        sq_st = flat_tmp[:, 7 * P:9 * P]

        acc = ctx.enter_context(nc.psum_tensor("acc", [P, MT, 512], F32))
        aux = ctx.enter_context(nc.psum_tensor("aux", [P, 4, 512], F32))

        x_in = [sem(f"x_in{t}") for t in range(3)]
        small_in = sem("small_in")
        state_in = sem("state_in")
        pages_in = sem("pages_in")
        raw_in = [sem(f"raw_in{r}") for r in range(RAW)]
        page_in = [sem(f"page_in{r}") for r in range(PG)]
        consts = sem("consts")
        causal_ok = sem("causal_ok")
        x_turned = sem("x_turned")
        x_kept = sem("x_kept")
        a_hi_ok = sem("a_hi_ok")
        a_lo_ok = sem("a_lo_ok")
        set_t = sem("set_t")
        set_v = sem("set_v")
        sq_x = sem("sq_x")
        hi_ok = sem("hi_ok")
        lo_ok = sem("lo_ok")
        w_used = sem("w_used")
        acc_ok = sem("acc_ok")
        acc_free = sem("acc_free")
        nrm_sq = sem("nrm_sq")
        nrm_sum = sem("nrm_sum")
        nrm_root = sem("nrm_root")
        nrm_v = sem("nrm_v")
        sn_mm = sem("sn_mm")
        sn_ok = sem("sn_ok")
        kT_mm = [sem("kT_mm0"), sem("kT_mm1")]
        kT_ok = [sem("kT_ok0"), sem("kT_ok1")]
        qc_ok = sem("qc_ok")
        sc_mm = sem("sc_mm")
        s_ev = sem("s_ev")
        s_mx = sem("s_mx")
        nm_ok = sem("nm_ok")
        pe_go = sem("pe_go")
        act_go = sem("act_go")
        exp_ok = sem("exp_ok")
        sel_v = sem("sel_v")
        pt_mm = sem("pt_mm")
        pt_a = sem("pt_a")
        pt_d = sem("pt_d")
        an_mm = sem("an_mm")
        sn_t = sem("sn_t")
        sn_a = sem("sn_a")
        an_ok = sem("an_ok")
        pv_mm = sem("pv_mm")
        or_ok = sem("or_ok")
        ex_mm = sem("ex_mm")
        o_ok = sem("o_ok")
        gate_e = sem("gate_e")
        gate_v = sem("gate_v")
        nat_mm = sem("nat_mm")
        nat_a = sem("nat_a")
        lam_v = sem("lam_v")
        lam_a = sem("lam_a")
        lam_m = sem("lam_m")
        sq_ok = sem("sq_ok")
        sv_ok = sem("sv_ok")
        zq_ok = sem("zq_ok")
        pa_s = sem("pa_s")
        pa_max = sem("pa_max")
        pa_exp = sem("pa_exp")
        pa_v = sem("pa_v")
        pa_t = sem("pa_t")
        pa_tc = sem("pa_tc")
        pa_o = sem("pa_o")
        pa_oc = sem("pa_oc")
        nw_m = sem("nw_m")
        nw_v = sem("nw_v")
        sub_sq = sem("sub_sq")
        sub_mm = sem("sub_mm")
        sub_rt = sem("sub_rt")
        sub_v = sem("sub_v")
        cv_p = sem("cv_p")
        cv_s = sem("cv_s")
        ln_mm = sem("ln_mm")
        ln_v = sem("ln_v")
        ln_sq = sem("ln_sq")
        ln_rt = sem("ln_rt")
        ln_n = sem("ln_n")
        ln_s = sem("ln_s")
        ln_e = sem("ln_e")
        x2_sq = sem("x2_sq")
        x2_mm = sem("x2_mm")
        x2_rt = sem("x2_rt")
        x2_v = sem("x2_v")
        up_h = sem("up_h")
        h_hi_ok = sem("h_hi_ok")
        h_lo_ok = sem("h_lo_ok")
        y_mm = sem("y_mm")
        y_a = sem("y_a")
        y_d = sem("y_d")
        v_out = sem("v_out")
        kc_out = sem("kc_out")
        y_out = sem("y_out")

        kin, kout = cache_k[0], cache_v[0]
        k_pages = kin.rearrange("n p h d -> n p (h d)")
        v_pages = kout.rearrange("n p h d -> n p (h d)")
        st = state_conv[0]
        n_phys = k_pages.shape[0]
        xs_rows = x_sample.rearrange("b t d -> (b t) d")
        w_in2, w_out2, w_up2, w_down2 = w_in[0], w_out[0], w_up[0], w_down[0]

        def w_chunk(w, row, col):
            return w[ds(row, CK * P), ds(col, VC)].rearrange("(k p) n -> p k n", p=P)

        block = ctx.enter_context(nc.Block())

        @block.sync
        def _(sp):
            def load_w(n, j, src):
                sp.wait_ge(lo_ok, NC * n + j + 1)
                sp.dma_start(raw[:, j % RAW], src).then_inc(raw_in[j % RAW], 16)

            def w_src(n, j):
                return w_chunk(w_in2, CK * P * j, VC * n)

            def load_page(s, j, keys, wait=None):
                r = sp.value_load(pages_sb[0:1, ds(N_PAGES * s + j, 1)], min_val=0, max_val=n_phys - 1)
                src = k_pages if keys else v_pages
                slot = j % KR + (0 if keys else KR)
                if wait:
                    sp.wait_ge(*wait)
                sp.dma_start(page[:, slot], src[ds(r, 1)].rearrange("a p n -> p (a n)"))\
                  .then_inc(page_in[slot], 16)

            xp = x_prompt[0]
            sp.dma_start(x_nat[0:N_META, 0, :], meta_tokens).then_inc(x_in[0], 16)
            sp.dma_start(x_nat[N_META:P, 0, :], xp[0:P - N_META, :]).then_inc(x_in[0], 16)
            sp.dma_start(x_nat[:, 1, :], xp[P - N_META:2 * P - N_META, :]).then_inc(x_in[1], 16)
            sp.dma_start(x_nat[0:16, 2, :], xp[2 * P - N_META:SEQ, :]).then_inc(x_in[2], 16)
            sp.dma_start(x_nat[16:48, 2, :], xs_rows).then_inc(x_in[2], 16)
            for j in range(RAW):
                load_w(0, j, w_src(0, j))
            for j in range(RAW, NC):
                load_w(0, j, w_src(0, j))
            with sp.Fori(1, ATT_FIRST) as n:
                for j in range(NC):
                    load_w(n, j, w_src(n, j))
            sp.wait_ge(x_turned, KT)
            sp.wait_ge(set_t, 6)
            sp.wait_ge(sq_x, 3)
            sp.wait_ge(pages_in, 16)
            for j in range(RAW):
                load_w(ATT_FIRST, j, w_src(ATT_FIRST, j))

            def body(ks, vs, n, nxt=None, first=False):
                for j in range(N_PAGES + 2):
                    if ks is not None and j < N_PAGES:
                        load_page(ks, j, True, None if first and j < KR else (kT_mm[1], N_PAGES * ks + j - KR + 1))
                    if vs is not None and j >= 2:
                        i = j - 2
                        load_page(vs, i, False, (pv_mm, KR + N_PAGES * vs + i - KR + 1))
                    if n is not None and j % 2 == 1 and j < N_PAGES:
                        c = (j - 1) // 2 + RAW
                        if c < NC:
                            load_w(n, c, w_src(n, c))
                        else:
                            load_w(n + 1, c - NC, nxt(n + 1, c - NC))

            def w_out_src(n, j):
                return w_chunk(w_out2, CK * P * j, VC * (n - OUT_V0))

            def first_out_src(n, j):
                return w_chunk(w_out2, CK * P * ((j + NC // 2) % NC), 0)

            body(0, None, ATT_FIRST, w_src, first=True)
            with sp.Fori(0, PAIR_V - 1) as s:
                body(s + 1, s, s + ATT_FIRST + 1, w_src)
            body(PAIR_V, PAIR_V - 1, Q_V - 1, first_out_src)
            with sp.Fori(PAIR_V, N_SEQ - 1) as s:
                body(s + 1, s, None)
            body(None, N_SEQ - 1, None)

            for j in range(RAW, NC):
                load_w(OUT_V0, j, first_out_src(OUT_V0, j))
            with sp.Fori(OUT_V0 + 1, MLP_V0) as n:
                for j in range(NC):
                    load_w(n, j, w_out_src(n, j))
            with sp.Fori(0, N_QTR) as q:
                with sp.Fori(0, UP_N) as u:
                    for j in range(NC):
                        load_w(MLP_V0 + q * QTR_N + u, j, w_chunk(w_up2, CK * P * j, q * FQ + u * VC))
                with sp.Fori(0, DOWN_N) as d:
                    for j in range(NC):
                        load_w(MLP_V0 + UP_N + q * QTR_N + d, j,
                               w_chunk(w_down2, q * FQ + CK * P * j, d * VC))
            for g in range(4):
                cols = slice(VC * g, VC * (g + 1))
                for i in range(3):
                    b = 3 * g + i
                    sp.wait_ge(y_a if b % 2 == 0 else y_d, b // 2 + 1)
                    if i < 2:
                        sp.dma_start(y_prompt[0, P * i:P * (i + 1), cols], y_nat[:, i, cols]).then_inc(y_out, 16)
                    else:
                        sp.dma_start(y_sample.rearrange("b t d -> (b t) d")[:, cols], y_smp[:, cols])\
                          .then_inc(y_out, 16)
            sp.wait_ge(y_out, 16 * 12)
            sp.wait_ge(v_out, 16 * 4)
            sp.wait_ge(kc_out, 16 * KC_STORES)

        @block.gpsimd
        def _(pool):
            def row(v):
                return v.rearrange("(a n) -> a n", n=P)
            pool.dma_start(vec_nat[V_ATTN:V_ATTN + 16, :], row(attn_norm[0])).then_inc(small_in, 16)
            pool.dma_start(vec_nat[V_MLP:V_MLP + 16, :], row(mlp_norm[0])).then_inc(small_in, 16)
            pool.dma_start(vec_nat[V_DWB:V_DWB + 8, :], row(dw_b[0])).then_inc(small_in, 16)
            pool.dma_start(vec_nat[V_LNG:V_LNG + 8, :], row(conv_ln_g[0])).then_inc(small_in, 16)
            pool.dma_start(vec_nat[V_LNB:V_LNB + 8, :], row(conv_ln_b[0])).then_inc(small_in, 16)
            pool.dma_start(vec_nat[V_SUB:V_SUB + 1, :], attn_subln).then_inc(small_in, 16)
            for half in range(2):
                pool.dma_start(vec_nat[V_Q:V_Q + 1, HD * half:HD * (half + 1)], q_norm).then_inc(small_in, 16)
                pool.dma_start(vec_nat[V_K:V_K + 1, HD * half:HD * (half + 1)], k_norm).then_inc(small_in, 16)
            pool.memset(ident[:], 0.0).then_inc(consts, 1)
            pool.memset(new_mask[:], 0.0).then_inc(consts, 1)
            pool.memset(head_ones[:], 0.0).then_inc(consts, 1)
            pool.memset(ones[:], 1.0).then_inc(consts, 1)
            pool.memset(eps[:], EPS).then_inc(consts, 1)
            pool.wait_ge(consts, 5)
            pool.affine_select(out=ident[:], in_=ident[:], compare_op=ALU.not_equal, fill=1.0, base=0,
                               pattern=[[-1, P]], channel_multiplier=1).then_inc(consts, 1)
            pool.affine_select(out=new_mask[:], in_=new_mask[:], compare_op=ALU.is_ge, fill=NEG_INF, base=0,
                               pattern=[[-DEC, N_SEQ], [0, DEC]], channel_multiplier=1).then_inc(consts, 1)
            pool.wait_ge(consts, 7)
            pool.memset(head_ones[0:HD, 0:HD], 1.0).then_inc(consts, 1)
            pool.wait_ge(consts, 8)
            pool.memset(head_ones[HD:P, HD:P], 1.0).then_inc(consts, 1)
            pool.wait_ge(consts, 9)
            pool.affine_select(out=new_mask[:], in_=new_mask[:], compare_op=ALU.is_ge, fill=NEG_INF, base=0,
                               pattern=[[DEC, N_SEQ], [1, DEC]], channel_multiplier=-1).then_inc(consts, 1)
            pool.memset(q_cur[:], 0.0).then_inc(consts, 1)
            pool.memset(pick[:], 0.0).then_inc(consts, 1)
            pool.wait_ge(consts, 12)
            pool.affine_select(out=pick[:], in_=pick[:], compare_op=ALU.not_equal, fill=1.0, base=0,
                               pattern=[[-DEC, 2], [-QC, N_H], [-1, DEC]], channel_multiplier=1).then_inc(consts, 1)
            for b in range(2):
                for s in range(4):
                    pool.dma_start(st_nat[30 * s:30 * (s + 1), b, :], st[4 * b + s]).then_inc(state_in, 16)
            pool.dma_start(cw_nat[:, :], dw_w[0]).then_inc(state_in, 16)
            pool.dma_start(pages_sb[0:1, :], page_table.rearrange("s (a n) -> a (s n)", a=1)).then_inc(pages_in, 16)
            for i, v in enumerate((lambda_q1, lambda_q2, lambda_k1, lambda_k2)):
                pool.dma_start(lam_in[0:1, i, :], v).then_inc(state_in, 16)

            kp = k_prompt[0, 0].rearrange("t h d -> t (h d)")
            vp = v_prompt[0, 0].rearrange("t h d -> t (h d)")
            ks = k_sample[0].rearrange("b t h d -> (b t) (h d)")
            vs = v_sample[0].rearrange("b t h d -> (b t) (h d)")
            for s in range(N_SEQ):
                pool.dma_start(conv_sample[0, s, 0:TAPS - 1 - DEC, :], st[s, DEC:TAPS - 1, :]).then_inc(kc_out, 16)

            def store(which, buf, prompt, smp, signal):
                for i, (t0, n) in enumerate(NAT):
                    pool.wait_ge(nat_a, 2 * (4 * which + i + 1))
                    dst = prompt[t0:t0 + n, :] if i < 3 else smp
                    slot = i if which else (i + 1) % 4
                    pool.dma_start(dst, buf[0:n, slot, :]).then_inc(signal, 16)

            pool.wait_ge(acc_ok, MT * Q_V)
            pool.memset(causal[:], 0.0).then_inc(causal_ok, 1)
            pool.wait_ge(causal_ok, 1)
            pool.affine_select(out=causal[:], in_=causal[:], compare_op=ALU.is_ge, fill=NEG_INF, base=0,
                               pattern=[[-1, P]], channel_multiplier=1).then_inc(causal_ok, 1)
            store(0, v_nat, vp, vs, v_out)
            store(1, k_nat, kp, ks, kc_out)
            pool.wait_ge(nat_a, 20)
            pool.dma_start(conv_prompt[0, 0], k_nat[64 - (TAPS - 1):64, 2, :]).then_inc(kc_out, 16)
            for s in range(N_SEQ):
                pool.dma_start(conv_sample[0, s, TAPS - 1 - DEC:TAPS - 1, :], k_nat[32 + DEC * s:32 + DEC * s + DEC, 3, :])\
                    .then_inc(kc_out, 16)
            pool.wait_ge(gate_v, 24)
            pool.wait_ge(set_v, 9)
            pool.tensor_copy(ext[:, :, :, TAPS - 1:], z[:, 24:32, PAD + T_P:ZW].rearrange("p c (s t) -> p c s t", t=DEC))\
                .then_inc(cv_s, 1)
            full = [P, 8, N_SEQ, DEC]
            bias = vec[:, V_DWB:V_DWB + 8].unsqueeze(2).unsqueeze(3).to_broadcast(full)
            pool.wait_ge(nat_mm, 8)
            pool.tensor_copy(c_smp, bias).then_inc(cv_s, 1)
            for j in range(TAPS):
                tap = taps[:, :, j:j + 1].unsqueeze(3).to_broadcast(full)
                pool.wait_ge(cv_s, 2 + 2 * j)
                pool.tensor_tensor(c_prod[:], ext[:, :, :, j:j + DEC], tap, ALU.mult).then_inc(cv_s, 1)
                pool.wait_ge(cv_s, 3 + 2 * j)
                pool.tensor_tensor(c_smp, c_smp, c_prod[:], ALU.add).then_inc(cv_s, 1)
        @block.tensor
        def _(pe):
            mm, transpose = nc.tensor.matmul, nc.tensor.transpose
            pe.sem_inc(sc_mm, 2)
            pe.sem_inc(pv_mm, KR)
            pe.sem_inc(x2_mm, 1)

            def products(n, kt, hi, lo, c0, width, tile=None):
                slot = kt // CK % SPL
                if kt % CK == 0:
                    pe.wait_ge(lo_ok, RAW + NC * n + kt // CK + 1)
                for m in range(MT):
                    if kt == 0:
                        pe.wait_ge(acc_free, MT * n + m + 1)
                    wh = w_hi[:, slot, kt % CK, P * m:P * (m + 1)]
                    wl = w_lo[:, slot, kt % CK, P * m:P * (m + 1)]
                    t = kt if tile is None else tile
                    ah, al = hi[:, t, c0:c0 + width], lo[:, t, c0:c0 + width]
                    out = acc[:, m, 0:width]
                    mm(out, wh, ah, start=(kt == 0), stop=False)
                    mm(out, wh, al, start=False, stop=False)
                    last = mm(out, wl, ah, start=False, stop=(kt == KT - 1))
                    if kt == KT - 1:
                        last.then_inc(acc_ok, 1)
                    elif kt % CK == CK - 1 and m == MT - 1:
                        last.then_inc(w_used, 1)

            pe.wait_ge(consts, CONSTS)
            pe.wait_ge(small_in, 160)
            transpose(aux[:, 0, 0:N_VEC], vec_nat[:, :], ident[0:N_VEC, 0:N_VEC]).then_inc(set_t, 1)
            for t in range(3):
                pe.wait_ge(x_in[t], 16 if t == 1 else 32)
            for kt in range(KT):
                if kt >= 4:
                    pe.wait_ge(x_kept, kt - 3)
                for t, (t0, n) in enumerate(TOK):
                    last = transpose(acc[:, kt % 4, t0:t0 + n], x_nat[0:n, t, P * kt:P * (kt + 1)],
                                     ident[0:n, 0:n])
                last.then_inc(x_turned, 1)
            pe.wait_ge(x_kept, KT)
            for kt in range(KT):
                pe.wait_ge(a_lo_ok, kt + 1)
                products(0, kt, a_hi, a_lo, 0, T)
                if kt == 3:
                    pe.wait_ge(state_in, STATE)
                    for c in range(8):
                        last = transpose(aux[:, 1, TAPS * c:TAPS * (c + 1)], cw_nat[:, P * c:P * (c + 1)],
                                         ident[0:TAPS, 0:TAPS])
                    last.then_inc(set_t, 1)
                    for g in range(4):
                        if g >= 2:
                            pe.wait_ge(set_v, 3 + g)
                        for c in range(4):
                            ch = 4 * (g % 2) + c
                            last = transpose(aux[:, (2, 3, 1, 2)[g], 120 * c:120 * (c + 1)],
                                             st_nat[:, g // 2, P * ch:P * (ch + 1)], ident[0:120, 0:120])
                        last.then_inc(set_t, 1)
                if kt == 8:
                    pe.wait_ge(set_v, 14)
                    for t, (t0, n) in enumerate(TOK):
                        last = mm(aux[:, 0, t0:t0 + n], rb[0:n, t, :], ident[0:n, 0:n], start=True, stop=True)
                    last.then_inc(set_t, 1)
            with pe.Fori(1, ATT_FIRST) as n:
                for kt in range(KT):
                    products(n, kt, a_hi, a_lo, 0, T)
                    if kt == 3:
                        for m in range(MT):
                            pe.wait_ge(nrm_sq, MT * (n - 1) + m + 1)
                            mm(aux[:, m, 0:T], head_ones[:], tmp[:, m, :], start=True, stop=True)\
                              .then_inc(nrm_sum, 1)
            pe.wait_ge(nrm_v, 1 + 2 * MT * NORM_VISITS)
            for h in range(N_H):
                for i in range(2):
                    rows = slice(HD * i, HD * (i + 1))
                    last = mm(aux[0:N_SMP, i, 0:N_SEQ * N_H * DEC].rearrange("p (s h t) -> p s h t", h=N_H, t=DEC)[:, :, h, :],
                              z[rows, 8 + h, PAD + T_P:PAD + T],
                              z[rows, h, PAD + T_P:PAD + T].rearrange("p (s t) -> p s t", t=DEC), start=True, stop=True)
            last.then_inc(sn_mm, 1)
            pe.wait_ge(sn_ok, 2)
            pe.wait_ge(lam_v, 4)
            mm(aux[:, 2, 0:1], ones[0:1, :], lam_one[0:1, :], start=True, stop=True).then_inc(lam_m, 1)
            pe.wait_ge(lam_v, 5)

            def turn_keys(s, j):
                pe.wait_ge(page_in[j % KR], 16 * (NG * s + j // KR + 1))
                for half in range(2):
                    pe.wait_ge(kT_ok[half], N_PAGES * s + j + 1)
                    for h in range(4):
                        last = transpose(aux[:, half, P * h:P * (h + 1)],
                                         page[:, j % KR, P * (4 * half + h):P * (4 * half + h + 1)], ident[:])
                    last.then_inc(kT_mm[half], 1)

            def score(s, j):
                pe.wait_ge(kT_ok[0], 1 + N_PAGES * s + j + 1)
                pe.wait_ge(kT_ok[1], 1 + N_PAGES * s + j + 1)
                if j == 0:
                    pe.wait_ge(qc_ok, 3 * (s + 1))
                if j % SG == 0:
                    pe.wait_ge(s_ev, NG * s + j // SG + 1)
                for h in range(N_H):
                    last = mm(aux[0:SC, 2, P * (j % SG):P * (j % SG + 1)], q_cur[:, SC * h:SC * (h + 1)],
                              kT[:, j % 2, h, :], start=(h == 0), stop=(h == N_H - 1))
                last.then_inc(sc_mm, 1)

            def turn_probs(s, half):
                if half == 0:
                    pe.wait_ge(o_ok, s + 1)
                else:
                    pe.wait_ge(pt_a, s + 1)
                for g in (2 * half, 2 * half + 1):
                    pe.wait_ge(exp_ok, (NG + 1) * s + g + 1)
                    pe.sem_inc(pe_go, 1)
                    for j in range(SG * g, SG * (g + 1)):
                        last = transpose(aux[:, 3, SC * (j % 8):SC * (j % 8 + 1)], s_rows[:, P * j:P * (j + 1)],
                                         ident[0:SC, 0:SC])
                    last.then_inc(pt_mm, 1)

            def new_keys(vs, ks):
                if vs is not None:
                    pe.wait_ge(pt_d, vs + 1)
                    pe.wait_ge(exp_ok, (NG + 1) * (vs + 1))
                    pe.wait_ge(sel_v, 3 * (vs + 1))
                    pe.sem_inc(pe_go, 1)
                    mm(aux[0:N_SMP, 3, SC:SC + N_H * DEC], s_rows[:, PAST:PAST + N_SMP],
                       pick_s[:].rearrange("p a c t -> p (a c t)"), start=True, stop=True).then_inc(an_mm, 1)
                if ks is not None:
                    pe.wait_ge(qc_ok, 3 * (ks + 1))
                    pe.sem_inc(pe_go, 1)
                    transpose(aux[0:SC, 3, 0:N_SMP], s_cur[:], ident[0:N_SMP, 0:N_SMP]).then_inc(sn_t, 1)

            def values(s, j, keys):
                pe.wait_ge(page_in[KR + j % KR], 16 * (NG * s + j // KR + 1))
                if j == 0:
                    pe.wait_ge(an_ok, s + 1)
                    if keys:
                        pe.wait_ge(sn_a, s + 2)
                for half in range(2):
                    rows = slice(SC // 2 * half, SC // 2 * (half + 1))
                    last = mm(aux[rows, 3, :], pT[:, j, rows], page[:, KR + j % KR, 512 * half:512 * (half + 1)],
                              start=(j == 0), stop=(j == N_PAGES - 1))
                last.then_inc(pv_mm, 1)

            def body(ks, vs, n, middle=None, end=None, finish=None):
                for j in range(N_PAGES):
                    if ks is not None:
                        turn_keys(ks, j)
                    if vs is not None and j < 2:
                        turn_probs(vs, j)
                    if j >= 1 and ks is not None:
                        score(ks, j - 1)
                    if j == 1:
                        new_keys(vs, ks)
                    if middle:
                        middle(j)
                    if n is not None:
                        products(n, j, a_hi, a_lo, 0, T)
                    if j >= 2 and vs is not None:
                        values(vs, j - 2, ks is not None)
                    if end:
                        end(j)
                if middle:
                    middle(N_PAGES)
                if ks is not None:
                    score(ks, N_PAGES - 1)
                if vs is not None:
                    values(vs, N_PAGES - 2, ks is not None)
                    values(vs, N_PAGES - 1, ks is not None)
                    if finish:
                        finish()
                    pe.wait_ge(or_ok, vs + 1)
                    for c in range(4):
                        last = mm(aux[:, 3, 0:N_H * DEC].rearrange("p (a c t) -> p a c t", a=2, c=4)[:, :, c, :],
                                  o_rows[:, P * c:P * (c + 1)], pick_s[:, :, c, :], start=True, stop=True)
                    last.then_inc(ex_mm, 1)

            body(0, None, ATT_FIRST)
            with pe.Fori(0, PAIR_V) as s:
                body(s + 1, s, s + ATT_FIRST + 1)
            pe.wait_ge(acc_free, MT * (Q_V + 1))
            b = 0
            for base, parts in ((16, NAT), (8, NAT), (24, ((T_P - 32, 32), (T_P, N_SMP)))):
                if base == 24:
                    pe.wait_ge(gate_v, 24)
                for t0, n in parts:
                    for half in range(2):
                        if b >= 4:
                            pe.wait_ge(nat_a, b - 3)
                        for h in range(4):
                            last = transpose(acc[0:n, b % 4, P * h:P * (h + 1)],
                                             z[:, base + 4 * half + h, PAD + t0:PAD + t0 + n], ident[:])
                        last.then_inc(nat_mm, 1)
                        b += 1
            pe.wait_ge(nat_a, 20)
            pe.wait_ge(causal_ok, 2)

            def p_score(u, h, blk):
                nk = N_META + P * (blk + 1)
                pe.wait_ge(sq_ok, 2 * (h + 1))
                pe.wait_ge(pa_exp, 1 + 2 * u)
                pe.sem_inc(pe_go, 1)
                for i in range(2):
                    for k0, k1 in ((0, nk - P), (nk - P, nk)):
                        mm(acc[:, i, k0:k1], q_st[:, i, P * blk:P * (blk + 1)],
                           z[:, ds(8 + h, 1), PAD + k0:PAD + k1].rearrange("p a t -> p (a t)"),
                           start=True, stop=(k0 == 0))
                    mm(acc[:, i, nk - P:nk], ident[:], causal[:], start=False, stop=True).then_inc(pa_s, 1)

            def key_tiles(blk):
                return [(0, P), (P, P), (2 * P, N_META)] if blk else [(0, P), (P, N_META)]

            def p_turn(u, blk):
                pe.wait_ge(pa_v, 4 * (u + 1))
                pe.wait_ge(pa_tc, 1 + 2 * u)
                for i, (k0, n) in enumerate(key_tiles(blk)):
                    last = transpose(acc[0:n, 2, P * i:P * (i + 1)], prob[:, 0, k0:k0 + n], ident[:])
                last.then_inc(pa_t, 1)

            def p_out(u, h, blk):
                tiles = key_tiles(blk)
                pe.wait_ge(pa_tc, 1 + 2 * (u + 1))
                pe.wait_ge(sv_ok, 2 * (h + 1))
                pe.wait_ge(pa_oc, 1 + u)
                pe.wait_ge(sub_rt, 1 + h)
                for i, (k0, n) in enumerate(tiles):
                    last = mm(acc[:, 3, 0:P], v_st[0:n, i, :], probT[0:n, i, :],
                              start=(i == 0), stop=(i == len(tiles) - 1))
                last.then_inc(pa_o, 1)

            def sub_sum(h):
                pe.wait_ge(sub_sq, h + 1)
                mm(acc[:, 3, P:3 * P], ones[:], sq_st, start=True, stop=True).then_inc(sub_mm, 1)

            with pe.Fori(ATT_S, ATT_S + 2) as s:
                u0, h0 = 2 * HB * (s - ATT_S), HB * (s - ATT_S)

                def out(k):
                    p_out(u0 + k, h0 + k // 2, k % 2)

                def middle(j):
                    if j % 2 == 0 and 2 <= j < N_PAGES:
                        p_turn(u0 + j // 2 - 1, (j // 2 - 1) % 2)
                        if j % 4 == 2 and j > 2:
                            sub_sum(h0 + j // 4 - 1)
                    elif j % 2 and j > 1:
                        out(j // 2 - 1)
                    elif j == N_PAGES:
                        out(N_PAGES // 2 - 1)

                def end(j):
                    k = j // 2
                    if j % 2 == 0:
                        p_score(u0 + k, h0 + k // 2, k % 2)
                    elif j == N_PAGES - 1:
                        p_turn(u0 + k, k % 2)

                body(s + 1, s, None, middle, end, finish=lambda: sub_sum(h0 + HB - 1))

            def layer_sums(j):
                if j == 3:
                    pe.wait_ge(cv_s, CV_S)
                    pe.wait_ge(cv_p, 8 * TAPS)
                    pe.wait_ge(pa_exp, 1 + 4 * N_H)
                    for c in range(8):
                        last = mm(acc[:, 0, 0:T_OUT], ones[:], z[:, 16 + c, 0:T_OUT], start=(c == 0), stop=(c == 7))
                    last.then_inc(ln_mm, 1)
                if j in (6, 7):
                    for c in range(4 * (j - 6), 4 * (j - 5)):
                        pe.wait_ge(ln_sq, c + 1)
                        last = mm(acc[:, 1, 0:T_OUT], ones[:], tmp[:, c % 4, 0:T_OUT], start=(c == 0), stop=(c == 7))
                        last.then_inc(ln_mm, 1)

            body(N_SEQ - 1, N_SEQ - 2, None, end=layer_sums)

            def new_values(j):
                if j == 3:
                    pe.wait_ge(an_ok, N_SEQ)
                    for h in range(N_H):
                        last = mm(aux[:, 1, 0:N_SEQ * N_H * DEC].rearrange("p (s h t) -> p s h t", h=N_H, t=DEC)[:, :, h, :],
                                  v_nat[0:N_SMP, 0, P * h:P * (h + 1)], a_new[:, :, DEC * h:DEC * (h + 1)],
                                  start=True, stop=True)
                    last.then_inc(nw_m, 1)

            def first_out(kt):
                pe.wait_ge(a_lo_ok, KT + kt + 1)
                products(OUT_V0, kt, a_hi, a_lo, 0, T_OUT, tile=(kt + 8) % KT)

            body(None, N_SEQ - 1, None, end=new_values, finish=lambda: first_out(0))
            first_out(1)
            pe.wait_ge(sub_sq, N_H + 1)
            mm(aux[:, 0, 0:2 * P], ones[:], flat_tmp[:, 0:2 * P], start=True, stop=True).then_inc(sub_mm, 1)
            for kt in range(2, KT):
                first_out(kt)

            def add_squares(i0, first=False, last=False):
                for m in range(MT):
                    pe.wait_ge(x2_sq, i0 + m + 1)
                    mm(aux[:, 0, 0:T_OUT], ones[:], tmp[:, m, 0:T_OUT], start=(first and m == 0),
                       stop=(last and m == MT - 1)).then_inc(x2_mm, 1)

            def out_visit(n, i0, first=False):
                for kt in range(KT):
                    products(n, kt, a_hi, a_lo, 0, T_OUT)
                    if kt == 7:
                        add_squares(i0, first)

            def up(n):
                for kt in range(KT):
                    products(n, kt, a_hi, a_lo, 0, T_OUT)

            def down(n, q):
                for kt in range(KT):
                    pe.wait_ge(h_lo_ok, KT * q + kt + 1)
                    products(n, kt, h_hi, h_lo, 0, T_OUT)

            out_visit(OUT_V0 + 1, 0, first=True)
            with pe.Fori(OUT_V0 + 2, MLP_V0) as n:
                out_visit(n, MT * (n - OUT_V0 - 1))
            for kt in range(KT):
                pe.wait_ge(a_lo_ok, 2 * KT + kt + 1)
                products(MLP_V0, kt, a_hi, a_lo, 0, T_OUT)
                if kt == 7:
                    add_squares(KT - MT, last=True)
            with pe.Fori(1, UP_N) as u:
                up(MLP_V0 + u)
            with pe.Fori(0, DOWN_N) as d:
                down(MLP_V0 + UP_N + d, 0)
            with pe.Fori(1, N_QTR) as q:
                with pe.Fori(0, UP_N) as u:
                    up(MLP_V0 + q * QTR_N + u)
                with pe.Fori(0, DOWN_N) as d:
                    down(MLP_V0 + UP_N + q * QTR_N + d, q)
            for g in range(4):
                pe.wait_ge(acc_free, MT + MT * (MLP_V0 + N_QTR * QTR_N - DOWN_N + g + 1))
                for i, (t0, n) in enumerate(((N_META, P), (N_META + P, P), (T_P, N_SMP))):
                    b = 3 * g + i
                    if b >= 4:
                        pe.wait_ge(y_a if b % 2 == 0 else y_d, (b - 4) // 2 + 1)
                    for m in range(MT):
                        last = transpose(aux[0:n, b % 4, P * m:P * (m + 1)], xT[:, MT * g + m, t0:t0 + n], ident[:])
                    last.then_inc(y_mm, 1)

        def free(eng, n, j):
            if j == 1:
                eng.wait_ge(acc_ok, MT * n)
            else:
                eng.wait_ge(w_used, (NC - 1) * n + max(j - 1, 0))

        @block.scalar
        def _(act):
            fn = nc.scalar.activation

            def hi(n, j):
                act.wait_ge(raw_in[j % RAW], 16 * (NC // RAW * n + j // RAW + 1))
                free(act, n, j)
                nc.scalar.copy(w_hi[:, j % SPL], raw[:, j % RAW]).then_inc(hi_ok, 1)

            def sqrt(out, in_, count):
                return fn(out, in_, ACT.Sqrt, scale=1.0 / count, bias=eps[0:out.shape[0], :])

            act.sem_inc(kT_ok[0], 1)
            act.sem_inc(s_ev, 1)
            act.sem_inc(pa_exp, 1)
            act.sem_inc(pa_tc, 1)
            act.sem_inc(sub_rt, 1)
            act.wait_ge(consts, CONSTS)
            act.wait_ge(set_v, 1)
            for kt in range(KT):
                act.wait_ge(x_kept, kt + 1)
                fn(a_hi[:, kt, :], xT[:, kt, :], ACT.Copy, scale=vec[:, V_ATTN + kt:V_ATTN + kt + 1])\
                    .then_inc(a_hi_ok, 1)
                if kt == 7:
                    hi(0, 0)
            hi(0, 1)
            for t, (_, n) in enumerate(TOK):
                act.wait_ge(x_in[t], 16 if t == 1 else 32)
                fn(z[0:n, 7 * t:7 * t + 7, :].rearrange("p a b -> p (a b)")[:, 0:D], x_nat[0:n, t, :], ACT.Square,
                   accum_out=sums[0:n, t:t + 1]).then_inc(sq_x, 1)
            act.wait_ge(sq_x, 3)
            sqrt(root[:, 0:2], sums[:, 0:2], D).then_inc(sq_x, 1)
            sqrt(root[0:48, 2:3], sums[0:48, 2:3], D).then_inc(sq_x, 1)
            for j in range(2, NC):
                hi(0, j)
            hi(1, 0)
            hi(1, 1)
            with act.Fori(1, ATT_FIRST) as n:
                for m in range(MT):
                    act.wait_ge(acc_free, MT + MT * (n - 1) + m + 1)
                    act.wait_ge(nrm_v, 1 + 2 * MT * (n - 1))
                    fn(tmp[:, m, :], z[:, ds(MT * (n - 1) + m, 1), PAD:ZW].rearrange("p a t -> p (a t)"),
                       ACT.Square).then_inc(nrm_sq, 1)
                for j in range(2, 4):
                    hi(n, j)
                for m in range(MT):
                    act.wait_ge(nrm_sum, MT * (n - 1) + m + 1)
                    sqrt(tmp[:, m, :], aux[:, m, 0:T], HD).then_inc(nrm_root, 1)
                for j in range(4, NC):
                    hi(n, j)
                hi(n + 1, 0)
                hi(n + 1, 1)

            act.wait_ge(lam_v, 2)
            fn(lam_exp[:], lam_sum[:], ACT.Exp).then_inc(lam_a, 1)

            def body(ks, vs, n, beside=None, after=None):
                def group(g):
                    act.wait_ge(sc_mm, 2 + N_PAGES * ks + SG * (g + 1))
                    if vs is not None:
                        act.wait_ge(pt_mm, NG * vs + g + 1)
                    nc.scalar.copy(s_rows[:, SG * P * g:SG * P * (g + 1)], aux[0:SC, 2, :]).then_inc(s_ev, 1)

                for j in range(N_PAGES):
                    if ks is not None:
                        act.wait_ge(kT_mm[0], N_PAGES * ks + j + 1)
                        act.wait_ge(sc_mm, N_PAGES * ks + j + 1)
                        nc.scalar.copy(kT[:, j % 2, 0:4, :], aux[:, 0, :].rearrange("p (h k) -> p h k", h=4))\
                            .then_inc(kT_ok[0], 1)
                    if ks is not None and n is None:
                        act.wait_ge(kT_mm[1], N_PAGES * ks + j + 1)
                        act.wait_ge(sc_mm, N_PAGES * ks + j + 1)
                        nc.scalar.copy(kT[:, j % 2, 4:8, :], aux[:, 1, :].rearrange("p (h k) -> p h k", h=4))\
                            .then_inc(kT_ok[1], 1)
                    if vs is not None and j == 0:
                        act.wait_ge(pt_mm, NG * vs + 2)
                        nc.scalar.copy(pT[:, 0:8, :], aux[:, 3, :].rearrange("p (j c) -> p j c", c=SC)).then_inc(pt_a, 1)
                    if ks is not None and j % SG == 0 and j:
                        group(j // SG - 1)
                    if n is not None and j % 2 == 0 and j:
                        if j < 14:
                            hi(n, j // 2 + 1)
                        else:
                            hi(n + 1, 0)
                    if beside:
                        beside(j)
                if beside:
                    beside(N_PAGES)
                if n is not None:
                    hi(n + 1, 1)
                if ks is not None:
                    group(NG - 1)
                    act.wait_ge(nm_ok, ks + 1)
                    for g in range(NG + 1):
                        keys = s_rows[:, SG * P * g:SG * P * (g + 1)] if g < NG else s_rows[:, PAST:PAST + N_SMP]
                        act.wait_ge(s_ev, 1 + NG * (ks + 1))
                        act.wait_ge(sn_a, ks + 1)
                        fn(keys, keys, ACT.Exp, bias=neg_max[:, 0:1], accum_out=s_sum[:, g:g + 1]).then_inc(exp_ok, 1)
                if after:
                    after()

            body(0, None, ATT_FIRST)
            with act.Fori(0, Z_VISITS - ATT_FIRST - 1) as s:
                body(s + 1, s, s + ATT_FIRST + 1)
            with act.Fori(Z_VISITS - ATT_FIRST - 1, PAIR_V) as s:
                n = s + ATT_FIRST + 1
                body(s + 1, s, n)
                for m in range(MT):
                    act.wait_ge(acc_free, MT + MT * n + m + 1)
                    fn(tmp[:, m, :], tmp[:, m, :], ACT.Exp, scale=-1.0).then_inc(gate_e, 1)
            b = 0
            for base, row, parts in ((16, 0, NAT), (8, 0, NAT), (24, 32, ((T_P - 32, 32), (T_P, N_SMP)))):
                for i, (_, n) in enumerate(parts):
                    buf, slot = (v_nat, (i + 1) % 4) if base == 16 else (k_nat, i if base == 8 else i + 2)
                    for half in range(2):
                        act.wait_ge(nat_mm, b + 1)
                        nc.scalar.copy(buf[row:row + n, slot, 512 * half:512 * (half + 1)], acc[0:n, b % 4, :])\
                            .then_inc(nat_a, 1)
                        b += 1

            def stage_q(h):
                act.wait_ge(zq_ok, 1)
                act.wait_ge(pa_exp, 1 + 4 * h)
                for i in range(2):
                    rows = slice(HD * i, HD * (i + 1))
                    nc.scalar.copy(q_st[rows, i, :],
                                   z[rows, ds(h, 1), PAD + N_META:PAD + T_P].rearrange("p a t -> p (a t)"))\
                        .then_inc(sq_ok, 1)

            def stage_v(h):
                act.wait_ge(pa_oc, 1 + 2 * h)
                nc.scalar.copy(v_st[:, 0:2, :], v_nat[:, 1:3, ds(P * h, P)]).then_inc(sv_ok, 1)
                nc.scalar.copy(v_st[0:N_META, 2, :], v_nat[0:N_META, 3, ds(P * h, P)]).then_inc(sv_ok, 1)

            def p_exp(u, blk):
                nk = N_META + P * (blk + 1)
                for i in range(2):
                    act.wait_ge(pa_max, 2 * u + i + 1)
                    fn(prob[:, i, 0:nk], acc[:, i, 0:nk], ACT.Exp, bias=pstat[:, i:i + 1],
                       accum_out=pstat[:, 2 + i:3 + i]).then_inc(pa_exp, 1)

            def p_copy(u, blk):
                full = blk + 1
                act.wait_ge(pa_t, u + 1)
                nc.scalar.copy(probT[:, 0:full, :], acc[:, 2, 0:P * full].rearrange("p (a q) -> p a q", q=P))\
                    .then_inc(pa_tc, 1)
                nc.scalar.copy(probT[0:N_META, full, :], acc[0:N_META, 2, P * full:P * (full + 1)]).then_inc(pa_tc, 1)

            def sub_square(h):
                act.wait_ge(pa_oc, 1 + 2 * (h + 1))
                act.sem_inc(act_go, 1)
                fn(sq_st, z[:, ds(h, 1), PAD + N_META:PAD + T_P].rearrange("p a t -> p (a t)"), ACT.Square)\
                    .then_inc(sub_sq, 1)

            def sub_root(h):
                act.wait_ge(sub_mm, h + 1)
                sqrt(sq_st, acc[:, 3, P:3 * P], P).then_inc(sub_rt, 1)

            with act.Fori(ATT_S, ATT_S + 2) as s:
                u0, h0 = 2 * HB * (s - ATT_S), HB * (s - ATT_S)

                def attend(j):
                    k = j // 2
                    if j % 2 == 0:
                        if j:
                            p_copy(u0 + k - 1, (k - 1) % 2)
                        if j % 4 == 2 and j > 2:
                            sub_root(h0 + j // 4 - 1)
                        if j % 4 == 0 and j < N_PAGES:
                            stage_q(h0 + j // 4)
                        if j % 4 == 2:
                            stage_v(h0 + j // 4)
                    else:
                        p_exp(u0 + k, k % 2)
                        if j % 4 == 1 and j > 1:
                            sub_square(h0 + j // 4 - 1)
                    if j == N_PAGES:
                        sub_square(h0 + HB - 1)

                def last_head():
                    sub_root(h0 + HB - 1)

                body(s + 1, s, None, attend, last_head)

            def layer_norm(j):
                if j in (5, 7):
                    for c in range(2 * (j - 5), 2 * (j - 5) + 4):
                        act.wait_ge(ln_v, c + 1)
                        if c >= 4:
                            act.wait_ge(ln_mm, 1 + c - 3)
                        fn(tmp[:, c % 4, 0:T_OUT], z[:, 16 + c, 0:T_OUT], ACT.Square).then_inc(ln_sq, 1)
                if j == 8:
                    act.wait_ge(ln_mm, 9)
                    sqrt(rstd[:, 0:T_OUT], acc[:, 1, 0:T_OUT], D_CONV).then_inc(ln_rt, 1)
                if 10 <= j < 14:
                    for c in (2 * (j - 10), 2 * (j - 10) + 1):
                        act.wait_ge(ln_n, 1 + 2 * (c + 1))
                        if c >= 4:
                            act.wait_ge(ln_s, 3 * (c - 3))
                        fn(tmp[:, c % 4, 0:T_OUT], z[:, 16 + c, 0:T_OUT], ACT.Exp, scale=-1.0).then_inc(ln_e, 1)

            body(N_SEQ - 1, N_SEQ - 2, None, layer_norm)

            def round_conv(j):
                if j == 2:
                    act.wait_ge(v_out, 16 * 4)
                    act.wait_ge(kc_out, 16 * KC_STORES)
                    act.wait_ge(ln_s, 3 * 8)
                    for c in range(8):
                        nc.scalar.copy(a_hi[:, 8 + c, 0:T_OUT], z[:, 16 + c, 0:T_OUT]).then_inc(a_hi_ok, 1)

            body(None, N_SEQ - 1, None, round_conv)
            act.wait_ge(nw_v, 1)
            fn(flat_tmp[:, 0:2 * P].rearrange("p (h t) -> p h t", h=N_H), z[:, 0:8, PAD + T_P:ZW], ACT.Square)\
                .then_inc(sub_sq, 1)
            act.wait_ge(sub_mm, N_H + 1)
            sqrt(flat_tmp[:, 0:2 * P], aux[:, 0, 0:2 * P], P).then_inc(sub_rt, 1)
            hi(OUT_V0, 2)

            def round_heads(j):
                if j < 7:
                    for h in (2 * (j - 3), 2 * (j - 3) + 1):
                        act.wait_ge(sub_v, 2 * N_H + 2)
                        nc.scalar.copy(a_hi[:, h, 0:T_OUT], z[:, h, PAD + N_META:ZW]).then_inc(a_hi_ok, 1)

            def visit(n, last=False, between=None, pre=3):
                for j in range(3, NC):
                    hi(n, j)
                    if between:
                        between(j)
                if not last:
                    for j in range(pre):
                        hi(n + 1, j)

            def squares(n, i0):
                for m in range(MT):
                    act.wait_ge(acc_free, MT + MT * n + m + 1)
                    act.wait_ge(x2_mm, 1 + i0)
                    fn(tmp[:, m, 0:T_OUT], xT[:, ds(i0 + m, 1), N_META:T].rearrange("p a t -> p (a t)"), ACT.Square)\
                        .then_inc(x2_sq, 1)

            def operand(kt):
                fn(a_hi[:, kt, 0:T_OUT], xT[:, kt, N_META:T], ACT.Copy, scale=vec[:, V_MLP + kt:V_MLP + kt + 1])\
                    .then_inc(a_hi_ok, 1)

            def operands(j):
                for kt in range(0 if j == 3 else CK * (j - 2), CK * (j - 1)):
                    operand(kt)

            visit(OUT_V0, between=round_heads)
            with act.Fori(OUT_V0 + 1, MLP_V0 - 1) as n:
                squares(n - 1, MT * (n - 1 - OUT_V0))
                visit(n)
            squares(MLP_V0 - 2, MT * (OUT_N - 2))
            visit(MLP_V0 - 1, between=operands)
            for kt in range(KT - MT, KT):
                act.wait_ge(acc_free, MT * (OUT_V0 + 1) + kt + 1)
                operand(kt)
            squares(MLP_V0 - 1, MT * (OUT_N - 1))

            def up(n, q, u, between=None):
                visit(n, between=between, pre=2)
                for m in range(MT):
                    if m == 2:
                        hi(n + 1, 2)
                    i = KT * q + MT * u + m
                    act.wait_ge(acc_free, MT + MT * n + m + 1)
                    fn(tmp[:, m, 0:T_OUT], tmp[:, m, 0:T_OUT], ACT.Square).then_inc(up_h, 1)
                    act.wait_ge(up_h, i + 1)
                    nc.scalar.copy(h_hi[:, ds(MT * u + m, 1), :].rearrange("p a t -> p (a t)"),
                                   tmp[:, m, 0:T_OUT]).then_inc(h_hi_ok, 1)

            def root_x2(j):
                if j == 4:
                    act.wait_ge(x2_mm, 1 + KT)
                    sqrt(rstd[:, 0:T_OUT], aux[:, 0, 0:T_OUT], D).then_inc(x2_rt, 1)

            up(MLP_V0, 0, 0, root_x2)
            with act.Fori(1, UP_N) as u:
                up(MLP_V0 + u, 0, u)
            with act.Fori(0, DOWN_N) as d:
                visit(MLP_V0 + UP_N + d)
            with act.Fori(1, N_QTR - 1) as q:
                with act.Fori(0, UP_N) as u:
                    up(MLP_V0 + q * QTR_N + u, q, u)
                with act.Fori(0, DOWN_N) as d:
                    visit(MLP_V0 + UP_N + q * QTR_N + d)
            n0 = MLP_V0 + (N_QTR - 1) * QTR_N
            with act.Fori(0, UP_N) as u:
                up(n0 + u, N_QTR - 1, u)
            with act.Fori(0, DOWN_N - 1) as d:
                visit(n0 + UP_N + d)
            visit(n0 + UP_N + DOWN_N - 1, last=True)
            for b in range(0, 12, 2):
                g, i = b // 3, b % 3
                n = P if i < 2 else N_SMP
                dst = y_nat[:, i, VC * g:VC * (g + 1)] if i < 2 else y_smp[:, VC * g:VC * (g + 1)]
                act.wait_ge(y_mm, b + 1)
                nc.scalar.copy(dst, aux[0:n, b % 4, :]).then_inc(y_a, 1)

        @block.vector
        def _(dve):
            v = nc.vector
            dve.sem_inc(lo_ok, RAW)
            dve.sem_inc(acc_free, MT)
            dve.sem_inc(kT_ok[1], 1)
            dve.sem_inc(o_ok, 1)
            dve.sem_inc(pa_oc, 1)
            dve.sem_inc(nrm_v, 1)

            def lo(n, j):
                dve.wait_ge(hi_ok, NC * n + j + 1)
                free(dve, n, j)
                v.tensor_tensor(w_lo[:, j % SPL], raw[:, j % RAW], w_hi[:, j % SPL].bitcast(F32), ALU.subtract)\
                    .then_inc(lo_ok, 1)

            def take(n, dst):
                for m in range(MT):
                    dve.wait_ge(acc_ok, MT * n + m + 1)
                    v.tensor_tensor(dst(m), acc[:, m, 0:T], rstd[:], ALU.mult).then_inc(acc_free, 1)

            def z_tile(i):
                return z[:, ds(i, 1), PAD:ZW].rearrange("p a t -> p (a t)")

            dve.wait_ge(set_t, 1)
            v.tensor_copy(vec[:], aux[:, 0, 0:N_VEC]).then_inc(set_v, 1)
            for kt in range(KT):
                dve.wait_ge(x_turned, kt + 1)
                v.tensor_copy(xT[:, kt, :], acc[:, kt % 4, 0:T]).then_inc(x_kept, 1)
                if kt >= 1:
                    k = kt - 1
                    dve.wait_ge(a_hi_ok, k + 1)
                    v.scalar_tensor_tensor(a_lo[:, k, :], xT[:, k, :], vec[:, V_ATTN + k:V_ATTN + k + 1],
                                           a_hi[:, k, :].bitcast(F32), ALU.mult, ALU.subtract).then_inc(a_lo_ok, 1)
                if kt == 9:
                    lo(0, 0)
            dve.wait_ge(a_hi_ok, KT)
            k = KT - 1
            v.scalar_tensor_tensor(a_lo[:, k, :], xT[:, k, :], vec[:, V_ATTN + k:V_ATTN + k + 1],
                                   a_hi[:, k, :].bitcast(F32), ALU.mult, ALU.subtract).then_inc(a_lo_ok, 1)
            lo(0, 1)
            v.memset(z[:, 24:32, 0:PAD], 0.0)
            v.tensor_scalar(vec[:, V_SUB:V_SUB + 1], vec[:, V_SUB:V_SUB + 1], 1.0 - LAMBDA_INIT, None, ALU.mult)\
                .then_inc(set_v, 1)
            v.tensor_scalar(qk_gain[:, 0:8], ones[:, 0:8], vec[:, V_Q:V_Q + 1], HD ** -0.5, ALU.mult, ALU.mult)\
                .then_inc(set_v, 1)
            v.tensor_scalar(qk_gain[:, 8:16], ones[:, 0:8], vec[:, V_K:V_K + 1], None, ALU.mult).then_inc(set_v, 1)
            dve.wait_ge(set_t, 2)
            v.tensor_copy(taps[:], aux[:, 1, 0:8 * TAPS].rearrange("p (c t) -> p c t", t=TAPS)).then_inc(set_v, 1)
            for g in range(4):
                dve.wait_ge(set_t, 3 + g)
                c0, s0 = 4 * (g % 2), 4 * (g // 2)
                v.tensor_copy(ext[:, c0:c0 + 4, s0:s0 + 4, 0:TAPS - 1],
                              aux[:, (2, 3, 1, 2)[g], 0:480].rearrange("p (c s t) -> p c s t", c=4, s=4))\
                    .then_inc(set_v, 1)
            lo(0, 2)
            dve.wait_ge(sq_x, 5)
            v.reciprocal(inv[:, 0:2], root[:, 0:2]).then_inc(set_v, 1)
            v.reciprocal(inv[0:48, 2:3], root[0:48, 2:3]).then_inc(set_v, 1)
            dve.wait_ge(set_v, 11)
            for t, (_, n) in enumerate(TOK):
                v.tensor_scalar(rb[0:n, t, :], ones[0:n, :], inv[0:n, t:t + 1], None, ALU.mult).then_inc(set_v, 1)
            for j in range(3, 6):
                lo(0, j)
            dve.wait_ge(set_t, 7)
            v.tensor_copy(rstd[:], aux[:, 0, 0:T]).then_inc(set_v, 1)
            dve.wait_ge(set_v, 15)
            for j in range(6, NC):
                lo(0, j)
            lo(1, 0)
            take(0, z_tile)
            lo(1, 1)
            with dve.Fori(1, ATT_FIRST) as n:
                for j in range(2, 4):
                    lo(n, j)
                done = 1 + 2 * MT * (n - 1)
                for m in range(MT):
                    lo(n, 4 + m)
                    dve.wait_ge(nrm_root, MT * (n - 1) + m + 1)
                    v.reciprocal(tmp[:, m, :], tmp[:, m, :]).then_inc(nrm_v, 1)
                lo(n + 1, 0)
                for m in range(MT):
                    dve.wait_ge(nrm_v, done + m + 1)
                    i = MT * (n - 1) + m
                    v.scalar_tensor_tensor(z_tile(i), z_tile(i), qk_gain[:, ds(i, 1)], tmp[:, m, :],
                                           ALU.mult, ALU.mult).then_inc(nrm_v, 1)
                take(n, lambda m: z_tile(MT * n + m))
                lo(n + 1, 1)
            dve.wait_ge(state_in, STATE)
            v.tensor_tensor(lam_prod[:], lam_in[:, 0:2, :], lam_in[:, 2:4, :], ALU.mult).then_inc(lam_v, 1)
            dve.wait_ge(lam_v, 1)
            v.tensor_reduce(lam_sum[:], lam_prod[:], AX, ALU.add).then_inc(lam_v, 1)
            dve.wait_ge(sn_mm, 1)
            for i in range(2):
                v.tensor_tensor(s_new[:, :, :, DEC * i:DEC * (i + 1)],
                                aux[0:N_SMP, i, 0:N_SEQ * N_H * DEC].rearrange("p (s h t) -> p s h t", h=N_H, t=DEC),
                                new_mask[:].unsqueeze(2).to_broadcast([N_SMP, N_SEQ, N_H, DEC]), ALU.add)\
                    .then_inc(sn_ok, 1)
            dve.wait_ge(lam_a, 1)
            v.tensor_tensor(lam_one[:], lam_exp[:, 0:1], lam_exp[:, 1:2], ALU.subtract).then_inc(lam_v, 1)
            dve.wait_ge(lam_v, 3)
            v.tensor_scalar(lam_one[:], lam_one[:], LAMBDA_INIT, None, ALU.add).then_inc(lam_v, 1)
            dve.wait_ge(lam_m, 1)
            v.tensor_scalar(neg_lam[:], aux[:, 2, 0:1], -1.0, None, ALU.mult).then_inc(lam_v, 1)
            dve.wait_ge(lam_v, 5)
            v.scalar_tensor_tensor(pick[:, 0], pick[:, 1], neg_lam[0:SC, 0:1], pick[:, 0], ALU.mult, ALU.add)\
                .then_inc(lam_v, 1)
            dve.wait_ge(lam_v, 6)

            def conv_tap(base, i, ch, j):
                def tile(t, c0):
                    return z[:, ds(t, 1), c0:c0 + SEQ].rearrange("p a t -> p (a t)")
                src, dst = tile(24 + ch, 2 + j), tile(16 + ch, 0)
                w = taps[:, ds(ch, 1), j:j + 1].rearrange("p a t -> p (a t)")
                if j == 0:
                    v.tensor_scalar(dst, src, w, vec[:, ds(V_DWB + ch, 1)], ALU.mult, ALU.add).then_inc(cv_p, 1)
                else:
                    v.scalar_tensor_tensor(dst, src, w, dst, ALU.mult, ALU.add).then_inc(cv_p, 1)

            def body(ks, vs, n, beside=None, finish=None):
                def group(g):
                    dve.wait_ge(s_ev, 1 + NG * ks + g + 1)
                    v.tensor_reduce(s_max[:, g:g + 1], s_rows[:, SG * P * g:SG * P * (g + 1)], AX, ALU.max)\
                        .then_inc(s_mx, 1)

                if ks is not None:
                    dve.wait_ge(sc_mm, 2 + N_PAGES * ks)
                    if vs is not None:
                        dve.wait_ge(sn_t, ks)
                    for i in range(2):
                        rows = slice(HD * i, HD * (i + 1))
                        v.tensor_copy(q_cur[rows, :].rearrange("p (h c) -> p h c", h=N_H)[:, :, DEC * i:DEC * (i + 1)],
                                      z[rows, 0:8, ds(PAD + T_P + DEC * ks, DEC)]).then_inc(qc_ok, 1)
                    v.tensor_copy(s_cur[:], s_new[:, ds(ks, 1)].rearrange("p a h c -> p (a h c)")).then_inc(qc_ok, 1)
                for j in range(N_PAGES):
                    if ks is not None and n is not None:
                        dve.wait_ge(kT_mm[1], N_PAGES * ks + j + 1)
                        dve.wait_ge(sc_mm, N_PAGES * ks + j + 1)
                        v.tensor_copy(kT[:, j % 2, 4:8, :], aux[:, 1, :].rearrange("p (h k) -> p h k", h=4))\
                            .then_inc(kT_ok[1], 1)
                    if j == 1:
                        if vs is not None:
                            dve.wait_ge(pt_mm, NG * vs + NG)
                            v.tensor_copy(pT[:, 8:16, :], aux[:, 3, :].rearrange("p (j c) -> p j c", c=SC))\
                                .then_inc(pt_d, 1)
                            dve.wait_ge(an_mm, vs + 1)
                            if ks is not None:
                                dve.wait_ge(sn_t, ks + 1)
                            v.tensor_copy(a_new[:, ds(vs, 1)].rearrange("p a c -> p (a c)"),
                                          aux[0:N_SMP, 3, SC:SC + N_H * DEC]).then_inc(an_ok, 1)
                        if ks is not None:
                            dve.wait_ge(sn_t, ks + 1)
                            v.tensor_copy(s_rows[:, PAST:PAST + N_SMP], aux[0:SC, 3, 0:N_SMP]).then_inc(sn_a, 1)
                    if ks is not None and j % SG == 0 and j:
                        group(j // SG - 1)
                    if n is not None and j % 2 == 0 and j:
                        if j < 14:
                            lo(n, j // 2 + 1)
                        else:
                            lo(n + 1, 0)
                    if beside:
                        beside(j)
                if beside:
                    beside(N_PAGES)
                if ks is not None:
                    group(NG - 1)
                    dve.wait_ge(sn_a, ks + 1)
                    v.tensor_reduce(s_max[:, NG:NG + 1], s_rows[:, PAST:PAST + N_SMP], AX, ALU.max).then_inc(s_mx, 1)
                    dve.wait_ge(s_mx, (NG + 1) * (ks + 1))
                    v.tensor_reduce(neg_max[:], s_max[:], AX, ALU.max, negate=True).then_inc(nm_ok, 1)
                if vs is not None:
                    dve.wait_ge(pv_mm, KR + N_PAGES * (vs + 1))
                    v.tensor_copy(o_rows[:], aux[0:SC, 3, :]).then_inc(or_ok, 1)
                if finish:
                    finish()
                if n is not None:
                    lo(n + 1, 1)
                if vs is not None:
                    dve.wait_ge(ex_mm, vs + 1)
                    v.tensor_copy(o_cache[:, ds(vs, 1), :].rearrange("p a c -> p (a c)"), aux[:, 3, 0:N_H * DEC])\
                        .then_inc(o_ok, 1)
                if ks is not None:
                    dve.wait_ge(exp_ok, (NG + 1) * (ks + 1))
                    v.tensor_reduce(l_inv[:, 0:1], s_sum[:], AX, ALU.add).then_inc(sel_v, 1)
                    dve.wait_ge(sel_v, 3 * ks + 1)
                    v.reciprocal(l_inv[:, 1:2], l_inv[:, 0:1]).then_inc(sel_v, 1)
                    dve.wait_ge(sel_v, 3 * ks + 2)
                    v.tensor_scalar(pick_s[:].rearrange("p a c t -> p (a c t)"),
                                    pick[:, 0].rearrange("p h t -> p (h t)"), l_inv[:, 1:2], None, ALU.mult)\
                        .then_inc(sel_v, 1)

            def take_z(n):
                take(n, lambda m: z_tile(MT * n + m))

            body(0, None, ATT_FIRST, finish=lambda: take_z(ATT_FIRST))
            with dve.Fori(0, Z_VISITS - ATT_FIRST - 1) as s:
                body(s + 1, s, s + ATT_FIRST + 1, finish=lambda: take_z(s + ATT_FIRST + 1))
            def gate(m):
                g, t = tmp[:, m % MT, :], z_tile(24 + m)
                dve.wait_ge(gate_e, m + 1)
                v.tensor_scalar(g, g, 1.0, None, ALU.add).then_inc(gate_v, 1)
                dve.wait_ge(gate_v, 3 * m + 1)
                v.reciprocal(g, g).then_inc(gate_v, 1)
                dve.wait_ge(gate_v, 3 * m + 2)
                v.tensor_tensor(t, t, g, ALU.mult).then_inc(gate_v, 1)

            def first_gates(j):
                if j % 3 == 1 and j // 3 < MT:
                    gate(j // 3)

            s0 = PAIR_V - 2
            body(s0 + 1, s0, Z_VISITS, finish=lambda: take(Z_VISITS, lambda m: tmp[:, m, :]))
            body(s0 + 2, s0 + 1, Z_VISITS + 1, first_gates, lambda: take(Z_VISITS + 1, lambda m: tmp[:, m, :]))
            for m in range(MT, 2 * MT):
                gate(m)

            dve.wait_ge(gate_v, 24)
            v.memset(q_st, 0.0).then_inc(zq_ok, 1)
            dve.wait_ge(nat_mm, 8)

            def p_max(u, blk):
                nk = N_META + P * (blk + 1)
                for i in range(2):
                    dve.wait_ge(pa_s, 2 * u + i + 1)
                    v.tensor_reduce(pstat[:, i:i + 1], acc[:, i, 0:nk], AX, ALU.max, negate=True).then_inc(pa_max, 1)

            def p_diff(u, blk):
                nk = N_META + P * (blk + 1)
                p1, p2 = prob[:, 0, 0:nk], prob[:, 1, 0:nk]
                dve.wait_ge(pa_exp, 1 + 2 * (u + 1))
                v.reciprocal(pstat[:, 2:4], pstat[:, 2:4]).then_inc(pa_v, 1)
                dve.wait_ge(pa_v, 4 * u + 1)
                v.tensor_tensor(pstat[:, 3:4], pstat[:, 3:4], neg_lam[:], ALU.mult).then_inc(pa_v, 1)
                v.tensor_scalar(p1, p1, pstat[:, 2:3], None, ALU.mult).then_inc(pa_v, 1)
                dve.wait_ge(pa_v, 4 * u + 3)
                v.scalar_tensor_tensor(p1, p2, pstat[:, 3:4], p1, ALU.mult, ALU.add).then_inc(pa_v, 1)

            def p_take(u, h, blk):
                c0 = PAD + N_META + P * blk
                dve.wait_ge(pa_o, u + 1)
                v.tensor_copy(z[:, ds(h, 1), c0:c0 + P].rearrange("p a t -> p (a t)"), acc[:, 3, 0:P]).then_inc(pa_oc, 1)

            def sub_norm(h):
                o = z[:, ds(h, 1), PAD + N_META:PAD + T_P].rearrange("p a t -> p (a t)")
                dve.wait_ge(sub_rt, 1 + h + 1)
                v.reciprocal(sq_st, sq_st).then_inc(sub_v, 1)
                dve.wait_ge(sub_v, 2 * h + 1)
                v.scalar_tensor_tensor(o, o, vec[:, V_SUB:V_SUB + 1], sq_st, ALU.mult, ALU.mult).then_inc(sub_v, 1)

            with dve.Fori(ATT_S, ATT_S + 2) as s:
                u0, h0 = 2 * HB * (s - ATT_S), HB * (s - ATT_S)
                work = iter([(i, i // CONV_S, i % CONV_S) for i in range(CONV_S * TAPS)])
                base = CONV_S * TAPS * (s - ATT_S)

                def conv(count):
                    for _ in range(count):
                        item = next(work, None)
                        if item:
                            i, j, c = item
                            if i >= CONV_S:
                                dve.wait_ge(cv_p, base + i - CONV_S + 1)
                            conv_tap(base, i, CONV_S * (s - ATT_S) + c, j)

                def take_unit(k):
                    p_take(u0 + k, h0 + k // 2, k % 2)

                def attend(j):
                    if j == N_PAGES:
                        take_unit(N_PAGES // 2 - 1)
                    elif j % 2 == 0:
                        conv(8)
                    else:
                        k = j // 2
                        p_max(u0 + k, k % 2)
                        if j > 1:
                            take_unit(k - 1)
                        conv(2)
                        p_diff(u0 + k, k % 2)
                        if j % 4 == 3 and j > 3:
                            sub_norm(h0 + j // 4 - 1)
                        conv(6)

                body(s + 1, s, None, attend)
                sub_norm(h0 + HB - 1)

            conv_t = [z[:, 16 + c, 0:T_OUT] for c in range(8)]

            def layer_norm(j):
                if j == 4:
                    dve.wait_ge(ln_mm, 1)
                    for c in range(8):
                        v.scalar_tensor_tensor(conv_t[c], acc[:, 0, 0:T_OUT], -1.0 / D_CONV, conv_t[c],
                                               ALU.mult, ALU.add).then_inc(ln_v, 1)
                if j == 9:
                    dve.wait_ge(ln_rt, 1)
                    v.reciprocal(rstd[:, 0:T_OUT], rstd[:, 0:T_OUT]).then_inc(ln_n, 1)
                    dve.wait_ge(ln_n, 1)
                    for c in range(8):
                        v.scalar_tensor_tensor(conv_t[c], conv_t[c], vec[:, V_LNG + c:V_LNG + c + 1],
                                               rstd[:, 0:T_OUT], ALU.mult, ALU.mult).then_inc(ln_n, 1)
                        dve.wait_ge(ln_n, 1 + 2 * c + 1)
                        v.tensor_scalar(conv_t[c], conv_t[c], vec[:, V_LNB + c:V_LNB + c + 1], None, ALU.add)\
                            .then_inc(ln_n, 1)
                if 11 <= j < 15:
                    for c in (2 * (j - 11), 2 * (j - 11) + 1):
                        e = tmp[:, c % 4, 0:T_OUT]
                        dve.wait_ge(ln_e, c + 1)
                        v.tensor_scalar(e, e, 1.0, None, ALU.add).then_inc(ln_s, 1)
                        dve.wait_ge(ln_s, 3 * c + 1)
                        v.reciprocal(e, e).then_inc(ln_s, 1)
                        dve.wait_ge(ln_s, 3 * c + 2)
                        v.tensor_tensor(conv_t[c], conv_t[c], e, ALU.mult).then_inc(ln_s, 1)

            body(N_SEQ - 1, N_SEQ - 2, None, layer_norm)

            def rest(i, tile, src):
                dve.wait_ge(a_hi_ok, KT + i + 1)
                v.tensor_tensor(a_lo[:, tile, 0:T_OUT], src, a_hi[:, tile, 0:T_OUT].bitcast(F32), ALU.subtract)\
                    .then_inc(a_lo_ok, 1)

            def rest_conv(j):
                if j == 2:
                    for c in range(8):
                        rest(c, 8 + c, conv_t[c])

            body(None, N_SEQ - 1, None, rest_conv)
            o_smp = z[:, 0:8, PAD + T_P:ZW]
            r_smp = flat_tmp[:, 0:2 * P]
            dve.wait_ge(nw_m, 1)
            dve.wait_ge(o_ok, 1 + N_SEQ)
            v.tensor_tensor(o_smp.rearrange("p h (s t) -> p s h t", t=DEC),
                            o_cache[:].rearrange("p s (h t) -> p s h t", t=DEC),
                            aux[:, 1, 0:N_SEQ * N_H * DEC].rearrange("p (s h t) -> p s h t", h=N_H, t=DEC), ALU.add)\
                .then_inc(nw_v, 1)
            dve.wait_ge(sub_rt, 1 + N_H + 1)
            v.reciprocal(r_smp, r_smp).then_inc(sub_v, 1)
            dve.wait_ge(sub_v, 2 * N_H + 1)
            v.scalar_tensor_tensor(o_smp, o_smp, vec[:, V_SUB:V_SUB + 1],
                                   r_smp.rearrange("p (h t) -> p h t", h=N_H), ALU.mult, ALU.mult).then_inc(sub_v, 1)
            lo(OUT_V0, 2)

            def rest_heads(j):
                if j < 7:
                    for h in (2 * (j - 3), 2 * (j - 3) + 1):
                        rest(8 + h, h, z[:, h, PAD + N_META:ZW])

            def add_x(n, i0):
                for m in range(MT):
                    x = xT[:, ds(i0 + m, 1), N_META:T].rearrange("p a t -> p (a t)")
                    dve.wait_ge(acc_ok, MT * n + m + 1)
                    v.tensor_tensor(x, x, acc[:, m, 0:T_OUT], ALU.add).then_inc(acc_free, 1)

            def visit(n, take_tiles, last=False, between=None, pre=3):
                for j in range(3, NC):
                    lo(n, j)
                    if between:
                        between(j)
                if not last:
                    lo(n + 1, 0)
                take_tiles()
                if not last:
                    for j in range(1, pre):
                        lo(n + 1, j)

            def operand(kt):
                dve.wait_ge(a_hi_ok, 2 * KT + kt + 1)
                v.scalar_tensor_tensor(a_lo[:, kt, 0:T_OUT], xT[:, kt, N_META:T], vec[:, V_MLP + kt:V_MLP + kt + 1],
                                       a_hi[:, kt, 0:T_OUT].bitcast(F32), ALU.mult, ALU.subtract)\
                    .then_inc(a_lo_ok, 1)

            def operands(j):
                for kt in range(0 if j == 3 else CK * (j - 2), CK * (j - 1)):
                    operand(kt)

            visit(OUT_V0, lambda: add_x(OUT_V0, 0), between=rest_heads)
            with dve.Fori(OUT_V0 + 1, MLP_V0 - 1) as n:
                visit(n, lambda: add_x(n, MT * (n - OUT_V0)))
            visit(MLP_V0 - 1, lambda: add_x(MLP_V0 - 1, MT * (OUT_N - 1)), between=operands)
            for kt in range(KT - MT, KT):
                operand(kt)

            def up(n, q, u, between=None):
                def take_up():
                    for m in range(MT):
                        dve.wait_ge(acc_ok, MT * n + m + 1)
                        v.scalar_tensor_tensor(tmp[:, m, 0:T_OUT], acc[:, m, 0:T_OUT], 0.0, rstd[:, 0:T_OUT],
                                               ALU.max, ALU.mult).then_inc(acc_free, 1)
                visit(n, take_up, between=between, pre=2)
                for m in range(MT):
                    if m == 2:
                        lo(n + 1, 2)
                    dve.wait_ge(h_hi_ok, KT * q + MT * u + m + 1)
                    t = lambda h: h[:, ds(MT * u + m, 1), :].rearrange("p a t -> p (a t)")
                    v.tensor_tensor(t(h_lo), tmp[:, m, 0:T_OUT], t(h_hi).bitcast(F32), ALU.subtract)\
                        .then_inc(h_lo_ok, 1)

            def invert_x2(j):
                if j == NC - 1:
                    dve.wait_ge(x2_rt, 1)
                    v.reciprocal(rstd[:, 0:T_OUT], rstd[:, 0:T_OUT]).then_inc(x2_v, 1)
                    dve.wait_ge(x2_v, 1)

            def down(n, d, last=False):
                visit(n, lambda: add_x(n, MT * d), last=last)

            up(MLP_V0, 0, 0, invert_x2)
            with dve.Fori(1, UP_N) as u:
                up(MLP_V0 + u, 0, u)
            with dve.Fori(0, DOWN_N) as d:
                down(MLP_V0 + UP_N + d, d)
            with dve.Fori(1, N_QTR - 1) as q:
                with dve.Fori(0, UP_N) as u:
                    up(MLP_V0 + q * QTR_N + u, q, u)
                with dve.Fori(0, DOWN_N) as d:
                    down(MLP_V0 + UP_N + q * QTR_N + d, d)
            n0 = MLP_V0 + (N_QTR - 1) * QTR_N
            with dve.Fori(0, UP_N) as u:
                up(n0 + u, N_QTR - 1, u)
            with dve.Fori(0, DOWN_N - 1) as d:
                down(n0 + UP_N + d, d)
            down(n0 + UP_N + DOWN_N - 1, DOWN_N - 1, last=True)
            for b in range(1, 12, 2):
                g, i = b // 3, b % 3
                n = P if i < 2 else N_SMP
                dst = y_nat[:, i, VC * g:VC * (g + 1)] if i < 2 else y_smp[:, VC * g:VC * (g + 1)]
                dve.wait_ge(y_mm, b + 1)
                v.tensor_copy(dst, aux[0:n, b % 4, :]).then_inc(y_d, 1)


_INS = ["x_prompt", "x_sample", "cache_k", "cache_v", "state_conv", "page_table", "meta_tokens", "attn_norm",
        "w_in", "q_norm", "k_norm", "lambda_q1", "lambda_k1", "lambda_q2", "lambda_k2", "attn_subln", "dw_w",
        "dw_b", "conv_ln_g", "conv_ln_b", "w_out", "mlp_norm", "w_up", "w_down"]
_OUTS = [(1, SEQ, D), (N_SEQ, DEC, D), (1, 1, T_P, 2 * N_H, HD), (1, 1, T_P, N_H, 2 * HD),
         (1, 1, TAPS - 1, D_CONV), (1, N_SEQ, DEC, 2 * N_H, HD), (1, N_SEQ, DEC, N_H, 2 * HD),
         (1, N_SEQ, TAPS - 1, D_CONV)]


def kernel(**inputs):
    import numpy as _np
    import concourse.bacc as _bacc
    from concourse.bass_utils import run_bass_kernel_spmd as _run

    nc = _bacc.Bacc("TRN2", target_bir_lowering=False, num_devices=1)
    arrays, args = {}, []
    for name in _INS:
        a = _np.ascontiguousarray(inputs[name])
        arrays[f"in_{name}"] = a
        args.append(nc.dram_tensor(f"in_{name}", a.shape, mybir.dt.from_np(a.dtype), kind="ExternalInput").ap())
    for i, shape in enumerate(_OUTS):
        args.append(nc.dram_tensor(f"out_{i}", shape, F32, kind="ExternalOutput").ap())
    build_step(nc, *args)
    r = _run(nc, [arrays], core_ids=[0])
    return tuple(r.results[0][f"out_{i}"] for i in range(len(_OUTS)))
```
